# Optimizing a Trainium2 kernel written in Bass

```python
import math
import jax, jax.numpy as jnp
from jax import lax
import numpy as np

D_MODEL = 1024
BATCH = 1
SEQ = 256
DEPTH = 1

RWKV_HEADS = 8
RWKV_HD = 64
RWKV_W = RWKV_HEADS * RWKV_HD
DECAY_LORA = 64
ICLR_LORA = 64
VRES_LORA = 32
GATE_LORA = 128
LNX_EPS = 64e-5
SB_HEADS = 8
SB_HD = 64
SB_W = SB_HEADS * SB_HD
SB_BLOCK = 128
MEM_LEN = 256
MEM_HEADS = 4
MEM_HD = 128
MEM_W = MEM_HEADS * MEM_HD
N_BRANCH = 3
BRANCH_W = 512
D_FF = 2816
CONV_W = 3
NORM_EPS = 1e-6

RWKV_SPLITS = (RWKV_W, RWKV_W, RWKV_W, DECAY_LORA, ICLR_LORA, GATE_LORA)
RWKV_COLS = sum(RWKV_SPLITS)
IN_COLS = RWKV_COLS + 3 * SB_W + MEM_W + N_BRANCH * D_MODEL


def rms_norm(x, g, eps=NORM_EPS):
    xf = x.astype(jnp.float32)
    y = xf * lax.rsqrt(jnp.mean(xf * xf, axis=-1, keepdims=True) + eps)
    return (y * g.astype(jnp.float32)).astype(x.dtype)

def split_heads(t, h, d):
    return t.reshape(t.shape[:-1] + (h, d))

def token_shift(p, mu):
    prev = jnp.pad(p, ((0, 0), (1, 0), (0, 0)))[:, :-1]
    return p + (prev - p) * mu

def rwkv7_recurrence(r, decay, k, v, kk, a):
    b, t, h, n = r.shape
    xs = tuple(jnp.moveaxis(z, 1, 0) for z in (r, decay, k, v, kk, a))

    def step(S, inp):
        r_t, w_t, k_t, v_t, kk_t, a_t = inp
        sa = jnp.einsum('bhij,bhj->bhi', S, -kk_t)
        S = (S * w_t[:, :, None, :]
             + sa[..., None] * (kk_t * a_t)[:, :, None, :]
             + v_t[..., None] * k_t[:, :, None, :])
        y_t = jnp.einsum('bhij,bhj->bhi', S, r_t)
        return S, y_t

    S0 = jnp.zeros((b, h, n, n), jnp.float32)
    _, ys = lax.scan(step, S0, xs)
    return jnp.moveaxis(ys, 0, 1)

def rwkv7_branch(p, mu, w0, w2, a0, a2, g2, k_k, k_a, r_k, lnx_g, lnx_b, v_first, vres):
    dt = p.dtype
    p = token_shift(p, mu)
    idx = list(np.cumsum(RWKV_SPLITS)[:-1])
    r, k, v, wl, al, gl = jnp.split(p, idx, axis=-1)
    f32 = jnp.float32
    w = -jax.nn.softplus(-(w0 + jnp.tanh(wl) @ w2).astype(f32)) - 0.5
    decay = jnp.exp(-jnp.exp(w))
    a = jax.nn.sigmoid((a0 + al @ a2).astype(f32))
    g = jax.nn.sigmoid(gl) @ g2
    if vres is None:
        v_first = v
    else:
        v0, v1, v2 = vres
        v = v + (v_first - v) * jax.nn.sigmoid(v0 + (v @ v1) @ v2)
    kk = split_heads((k * k_k).astype(f32), RWKV_HEADS, RWKV_HD)
    kk = kk / jnp.maximum(jnp.sqrt(jnp.sum(kk * kk, axis=-1, keepdims=True)), 1e-12)
    k = k.astype(f32) * (1.0 + (a - 1.0) * k_a.astype(f32))
    rh = split_heads(r.astype(f32), RWKV_HEADS, RWKV_HD)
    kh = split_heads(k, RWKV_HEADS, RWKV_HD)
    vh = split_heads(v.astype(f32), RWKV_HEADS, RWKV_HD)
    ah = split_heads(a, RWKV_HEADS, RWKV_HD)
    dh = split_heads(decay, RWKV_HEADS, RWKV_HD)
    y = rwkv7_recurrence(rh, dh, kh, vh, kk, ah)
    mean = jnp.mean(y, axis=-1, keepdims=True)
    var = jnp.mean(jnp.square(y - mean), axis=-1, keepdims=True)
    y = (y - mean) * lax.rsqrt(var + LNX_EPS)
    y = y.reshape(y.shape[:2] + (RWKV_W,)) * lnx_g.astype(f32) + lnx_b.astype(f32)
    bonus = jnp.sum(rh * kh * r_k.astype(f32), axis=-1, keepdims=True) * vh
    y = (y + bonus.reshape(y.shape)) * g.astype(f32)
    return y.astype(dt), v_first

def stick_breaking_attention(q, k, v):
    t_len = q.shape[2]
    scale = SB_HD ** -0.5
    outs = []
    for blk in range(t_len // SB_BLOCK):
        start = blk * SB_BLOCK
        end = start + SB_BLOCK
        qb = q[:, :, start:end]
        kb = k[:, :, :end]
        vb = v[:, :, :end]
        z = jnp.einsum('bhqd,bhkd->bhqk', qb, kb).astype(jnp.float32) * scale
        t_idx = start + jnp.arange(SB_BLOCK)
        s_idx = jnp.arange(end)
        mask = s_idx[None, :] < t_idx[:, None]
        log_1mb = jnp.where(mask, jax.nn.log_sigmoid(-z), 0.0)
        log_between = lax.cumsum(log_1mb, axis=3, reverse=True) - log_1mb
        attn = jnp.where(mask, jnp.exp(jax.nn.log_sigmoid(z) + log_between), 0.0)
        outs.append(jnp.einsum('bhqk,bhkd->bhqd', attn.astype(v.dtype), vb))
    return jnp.concatenate(outs, axis=2)

def stick_breaking_branch(p, q_g, k_g):
    b, t, _ = p.shape
    q, k, v = jnp.split(p, 3, axis=-1)
    q = rms_norm(split_heads(q, SB_HEADS, SB_HD), q_g).transpose(0, 2, 1, 3)
    k = rms_norm(split_heads(k, SB_HEADS, SB_HD), k_g).transpose(0, 2, 1, 3)
    v = split_heads(v, SB_HEADS, SB_HD).transpose(0, 2, 1, 3)
    o = stick_breaking_attention(q, k, v)
    return o.transpose(0, 2, 1, 3).reshape(b, t, SB_W)

def memory_branch(q, mem, mem_g, w_kv, q_g, k_g):
    b, t, _ = q.shape
    kv = rms_norm(mem, mem_g) @ w_kv
    mk, mv = jnp.split(kv, 2, axis=-1)
    qh = rms_norm(split_heads(q, MEM_HEADS, MEM_HD), q_g)
    kh = rms_norm(split_heads(mk, MEM_HEADS, MEM_HD), k_g)
    vh = split_heads(mv, MEM_HEADS, MEM_HD)
    s = jnp.einsum('bthd,bmhd->bhtm', qh, kh).astype(jnp.float32) * (MEM_HD ** -0.5)
    pr = jax.nn.softmax(s, axis=-1).astype(vh.dtype)
    o = jnp.einsum('bhtm,bmhd->bthd', pr, vh)
    return o.reshape(b, t, MEM_W)

def conv_ffn(x, g, w_up, conv_w, conv_b, w_down):
    h = rms_norm(x, g) @ w_up
    t = h.shape[1]
    hp = jnp.pad(h, ((0, 0), (CONV_W - 1, 0), (0, 0)))
    acc = conv_b + hp[:, 0:t] * conv_w[0]
    for i in range(1, CONV_W):
        acc = acc + hp[:, i:i + t] * conv_w[i]
    gate, val = jnp.split(acc, 2, axis=-1)
    return (jax.nn.silu(gate) * val) @ w_down

def first_inputs(seed: int = 0) -> dict:
    key = jax.random.key(seed)
    ks = jax.random.split(key, 40)
    f32 = jnp.float32
    nrm = lambda k, s, sc: jax.random.normal(k, s, f32) * sc
    gain = lambda k, s: 1.0 + 0.05 * jax.random.normal(k, s, f32)
    L = DEPTH
    return {
        "x": nrm(ks[0], (BATCH, SEQ, D_MODEL), 1.0),
        "mem": nrm(ks[1], (BATCH, MEM_LEN, D_MODEL), 1.0),
        "norm1_g": gain(ks[2], (L, D_MODEL)),
        "w_in": nrm(ks[3], (L, D_MODEL, IN_COLS), D_MODEL ** -0.5),
        "shift_mu": jax.random.uniform(ks[4], (L, RWKV_COLS), f32, 0.0, 1.0),
        "decay_w0": jax.random.uniform(ks[5], (L, RWKV_W), f32, -6.0, 1.0),
        "decay_w2": nrm(ks[6], (L, DECAY_LORA, RWKV_W), 0.5 * DECAY_LORA ** -0.5),
        "iclr_a0": nrm(ks[7], (L, RWKV_W), 0.1),
        "iclr_a2": nrm(ks[8], (L, ICLR_LORA, RWKV_W), ICLR_LORA ** -0.5),
        "gate_g2": nrm(ks[9], (L, GATE_LORA, RWKV_W), GATE_LORA ** -0.5),
        "k_k": 0.85 + 0.05 * jax.random.normal(ks[10], (L, RWKV_W), f32),
        "k_a": gain(ks[11], (L, RWKV_W)),
        "r_k": nrm(ks[12], (L, RWKV_HEADS, RWKV_HD), 0.1),
        "lnx_g": gain(ks[13], (L, RWKV_W)),
        "lnx_b": nrm(ks[14], (L, RWKV_W), 0.02),
        "vres_v0": 1.0 + 0.1 * jax.random.normal(ks[15], (L - 1, RWKV_W), f32),
        "vres_v1": nrm(ks[16], (L - 1, RWKV_W, VRES_LORA), RWKV_W ** -0.5),
        "vres_v2": nrm(ks[17], (L - 1, VRES_LORA, RWKV_W), VRES_LORA ** -0.5),
        "sb_q_norm_g": gain(ks[18], (L, SB_HD)),
        "sb_k_norm_g": gain(ks[19], (L, SB_HD)),
        "mem_norm_g": gain(ks[20], (L, D_MODEL)),
        "w_mem_kv": nrm(ks[21], (L, D_MODEL, 2 * MEM_W), D_MODEL ** -0.5),
        "mem_q_norm_g": gain(ks[22], (L, MEM_HD)),
        "mem_k_norm_g": gain(ks[23], (L, MEM_HD)),
        "w_branch": nrm(ks[24], (L, N_BRANCH, BRANCH_W, D_MODEL), BRANCH_W ** -0.5),
        "w_out": nrm(ks[25], (L, D_MODEL, D_MODEL), D_MODEL ** -0.5),
        "norm2_g": gain(ks[26], (L, D_MODEL)),
        "w_up": nrm(ks[27], (L, D_MODEL, 2 * D_FF), D_MODEL ** -0.5),
        "conv_w": nrm(ks[28], (L, CONV_W, 2 * D_FF), CONV_W ** -0.5),
        "conv_b": nrm(ks[29], (L, 2 * D_FF), 0.02),
        "w_down": nrm(ks[30], (L, D_FF, D_MODEL), D_FF ** -0.5),
    }

def first_block(x, mem, norm1_g, w_in, shift_mu, decay_w0, decay_w2, iclr_a0, iclr_a2, gate_g2,
              k_k, k_a, r_k, lnx_g, lnx_b, vres_v0, vres_v1, vres_v2, sb_q_norm_g, sb_k_norm_g,
              mem_norm_g, w_mem_kv, mem_q_norm_g, mem_k_norm_g, w_branch, w_out, norm2_g,
              w_up, conv_w, conv_b, w_down):
    b, t, _ = x.shape
    cut = [RWKV_COLS, RWKV_COLS + 3 * SB_W, RWKV_COLS + 3 * SB_W + MEM_W]
    v_first = None
    for l in range(DEPTH):
        h = rms_norm(x, norm1_g[l])
        proj = h @ w_in[l]
        p_rwkv, p_sb, q_mem, gate_logits = jnp.split(proj, cut, axis=-1)
        vres = None if l == 0 else (vres_v0[l - 1], vres_v1[l - 1], vres_v2[l - 1])
        y_a, v_first = rwkv7_branch(p_rwkv, shift_mu[l], decay_w0[l], decay_w2[l], iclr_a0[l],
                                    iclr_a2[l], gate_g2[l], k_k[l], k_a[l], r_k[l], lnx_g[l],
                                    lnx_b[l], v_first, vres)
        y_b = stick_breaking_branch(p_sb, sb_q_norm_g[l], sb_k_norm_g[l])
        y_m = memory_branch(q_mem, mem, mem_norm_g[l], w_mem_kv[l], mem_q_norm_g[l], mem_k_norm_g[l])
        ys = jnp.stack([y_a, y_b.astype(y_a.dtype), y_m.astype(y_a.dtype)], axis=2)
        branch_out = jnp.einsum('btnc,ncd->btnd', ys, w_branch[l])
        gates = jax.nn.sigmoid(gate_logits.reshape(b, t, N_BRANCH, D_MODEL))
        merged = jnp.sum(gates * branch_out, axis=2)
        x = x + merged @ w_out[l]
        x = x + conv_ffn(x, norm2_g[l], w_up[l], conv_w[l], conv_b[l], w_down[l])
    return x


DEPTH_2 = 2

N_A = DEPTH_2 // 2
N_B = DEPTH_2 - N_A
M_HEADS = 4
M_DQK = 128
M_DV = D_MODEL // M_HEADS
M_CHUNK = 64
M_SPLITS = [M_HEADS * M_DQK, 2 * M_HEADS * M_DQK, 2 * M_HEADS * M_DQK + M_HEADS * M_DV,
            2 * M_HEADS * M_DQK + 2 * M_HEADS * M_DV, 2 * M_HEADS * M_DQK + 2 * M_HEADS * M_DV + M_HEADS]
M_IN = 2 * M_HEADS * M_DQK + 2 * M_HEADS * M_DV + 2 * M_HEADS
A_HEADS = 8
A_DH = D_MODEL // A_HEADS
ROT_DIM = A_DH // 4
ROPE_THETA = 500000.0
MOBA_BLOCK = 256
MOBA_TOPK = 3
Q_BLOCK = 128
EPS = 1e-6


def rmsnorm(x, g):
    xf = x.astype(jnp.float32)
    y = xf * lax.rsqrt(jnp.mean(xf * xf, axis=-1, keepdims=True) + EPS)
    return (y * g.astype(jnp.float32)).astype(x.dtype)

def rope_tables(s_len):
    pos = jnp.arange(s_len, dtype=jnp.float32)
    inv = ROPE_THETA ** (-jnp.arange(0, ROT_DIM, 2, dtype=jnp.float32) / ROT_DIM)
    ang = pos[:, None] * inv[None, :]
    return jnp.cos(ang), jnp.sin(ang)

def apply_partial_rope(t, cos, sin):
    half = ROT_DIM // 2
    t1, t2, rest = t[..., :half], t[..., half:ROT_DIM], t[..., ROT_DIM:]
    c = cos[None, :, None, :].astype(t.dtype)
    s = sin[None, :, None, :].astype(t.dtype)
    return jnp.concatenate([t1 * c - t2 * s, t2 * c + t1 * s, rest], axis=-1)

def mlstm_chunkwise(q, k, v, i_pre, f_pre):
    b_, s_, h_, dk = q.shape
    nc = s_ // M_CHUNK

    def to_chunks(t):
        t = t.astype(jnp.float32).reshape((b_, nc, M_CHUNK, h_) + t.shape[3:])
        return jnp.moveaxis(jnp.moveaxis(t, 1, 0), 3, 2)

    qc, kc, vc = to_chunks(q), to_chunks(k), to_chunks(v)
    ic = to_chunks(i_pre)
    lfc = to_chunks(jax.nn.log_sigmoid(f_pre.astype(jnp.float32)))
    tri = jnp.tril(jnp.ones((M_CHUNK, M_CHUNK), dtype=bool))

    def step(carry, inp):
        c_st, n_st, m_st = carry
        qb, kb, vb, ib, lfb = inp
        bcum = jnp.cumsum(lfb, axis=-1)
        dmat = jnp.where(tri, bcum[..., :, None] - bcum[..., None, :] + ib[..., None, :], -jnp.inf)
        inter = bcum + m_st[..., None]
        m_t = jnp.maximum(inter, jnp.max(dmat, axis=-1))
        w_inter = jnp.exp(inter - m_t)
        s = jnp.einsum('bhtd,bhsd->bhts', qb, kb) * jnp.exp(dmat - m_t[..., None])
        num = w_inter[..., None] * jnp.einsum('bhtd,bhde->bhte', qb, c_st) + jnp.einsum('bhts,bhse->bhte', s, vb)
        den = w_inter * jnp.einsum('bhtd,bhd->bht', qb, n_st) + jnp.sum(s, axis=-1)
        h = num / jnp.maximum(jnp.abs(den), jnp.exp(-m_t))[..., None]
        b_last = bcum[..., -1]
        g = b_last[..., None] - bcum + ib
        m_new = jnp.maximum(b_last + m_st, jnp.max(g, axis=-1))
        decay = jnp.exp(b_last + m_st - m_new)
        wk = jnp.exp(g - m_new[..., None])[..., None] * kb
        c_new = decay[..., None, None] * c_st + jnp.einsum('bhsd,bhse->bhde', wk, vb)
        n_new = decay[..., None] * n_st + jnp.sum(wk, axis=-2)
        return (c_new, n_new, m_new), h

    dv = v.shape[-1]
    init = (jnp.zeros((b_, h_, dk, dv), jnp.float32), jnp.zeros((b_, h_, dk), jnp.float32),
            jnp.zeros((b_, h_), jnp.float32))
    _, hs = lax.scan(step, init, (qc, kc, vc, ic, lfc))
    return jnp.transpose(hs, (1, 0, 3, 2, 4)).reshape(b_, s_, h_, dv)

def mlstm_mixer(x, norm_g, w_in, b_gates, h_norm_g, w_out):
    b_, s_, _ = x.shape
    u = rmsnorm(x, norm_g) @ w_in
    q, k, v, o, gi, gf = jnp.split(u, M_SPLITS, axis=-1)
    q = q.reshape(b_, s_, M_HEADS, M_DQK) * (M_DQK ** -0.5)
    k = k.reshape(b_, s_, M_HEADS, M_DQK)
    v = v.reshape(b_, s_, M_HEADS, M_DV)
    i_pre = gi.astype(jnp.float32) + b_gates[0]
    f_pre = gf.astype(jnp.float32) + b_gates[1]
    h = mlstm_chunkwise(q, k, v, i_pre, f_pre)
    h = rmsnorm(h, h_norm_g.reshape(M_HEADS, M_DV)).reshape(b_, s_, M_HEADS * M_DV)
    h = h * jax.nn.sigmoid(o.astype(jnp.float32))
    return h.astype(x.dtype) @ w_out

def conv_ffn_2(x, norm_g, w_up, conv_w, conv_b, w_down):
    s_ = x.shape[1]
    u = rmsnorm(x, norm_g) @ w_up
    up = jnp.pad(u, ((0, 0), (CONV_W - 1, 0), (0, 0)))
    c = conv_b + up[:, 0:s_] * conv_w[0]
    for j in range(1, CONV_W):
        c = c + up[:, j:j + s_] * conv_w[j]
    val, gate = jnp.split(c, 2, axis=-1)
    return (jax.nn.silu(gate) * val) @ w_down

def shared_kv(x, norm_g, w_kv, k_norm_g, cos, sin):
    b_, s_, _ = x.shape
    kv = rmsnorm(x, norm_g) @ w_kv
    k, v = jnp.split(kv, 2, axis=-1)
    k = apply_partial_rope(rmsnorm(k.reshape(b_, s_, A_HEADS, A_DH), k_norm_g), cos, sin)
    v = v.reshape(b_, s_, A_HEADS, A_DH)
    nb = -(-s_ // MOBA_BLOCK)
    pad = nb * MOBA_BLOCK - s_
    k = jnp.pad(k, ((0, 0), (0, pad), (0, 0), (0, 0)))
    v = jnp.pad(v, ((0, 0), (0, pad), (0, 0), (0, 0)))
    kb = k.reshape(b_, nb, MOBA_BLOCK, A_HEADS, A_DH).transpose(0, 3, 1, 2, 4)
    vb = v.reshape(b_, nb, MOBA_BLOCK, A_HEADS, A_DH).transpose(0, 3, 1, 2, 4)
    kmean = jnp.mean(kb.astype(jnp.float32), axis=3).astype(kb.dtype)
    return kb, vb, kmean

def moba_mixer(x, norm_g, w_q, q_norm_g, w_o, kb, vb, kmean, cos, sin):
    b_, s_, _ = x.shape
    q = (rmsnorm(x, norm_g) @ w_q).reshape(b_, s_, A_HEADS, A_DH)
    q = apply_partial_rope(rmsnorm(q, q_norm_g), cos, sin) * (A_DH ** -0.5)
    q = q.transpose(0, 2, 1, 3)
    nb = kb.shape[2]
    n_topk = min(MOBA_TOPK, nb)
    bidx = jnp.arange(b_)[:, None, None, None]
    hidx = jnp.arange(A_HEADS)[None, :, None, None]
    n_sel = n_topk * MOBA_BLOCK

    def attend_block(qi):
        start = qi * Q_BLOCK
        cur = start // MOBA_BLOCK
        qb = lax.dynamic_slice_in_dim(q, start, Q_BLOCK, axis=2)
        gate = jnp.einsum('bhqd,bhnd->bhqn', qb, kmean).astype(jnp.float32)
        gate = jnp.where(jnp.arange(nb) < cur, gate, -jnp.inf)
        _, sel = lax.top_k(gate, n_topk)
        sel_valid = jnp.arange(n_topk) < cur
        kg = kb[bidx, hidx, sel]
        vg = vb[bidx, hidx, sel]
        l_sel = jnp.einsum('bhqd,bhqjkd->bhqjk', qb, kg).astype(jnp.float32)
        l_sel = jnp.where(sel_valid[:, None], l_sel, -jnp.inf).reshape(b_, A_HEADS, Q_BLOCK, n_sel)
        ko = lax.dynamic_index_in_dim(kb, cur, axis=2, keepdims=False)
        vo = lax.dynamic_index_in_dim(vb, cur, axis=2, keepdims=False)
        l_own = jnp.einsum('bhqd,bhkd->bhqk', qb, ko).astype(jnp.float32)
        qpos = start + jnp.arange(Q_BLOCK)
        kpos = cur * MOBA_BLOCK + jnp.arange(MOBA_BLOCK)
        l_own = jnp.where(kpos[None, :] <= qpos[:, None], l_own, -jnp.inf)
        p = jax.nn.softmax(jnp.concatenate([l_sel, l_own], axis=-1), axis=-1).astype(vb.dtype)
        p_sel = p[..., :n_sel].reshape(b_, A_HEADS, Q_BLOCK, n_topk, MOBA_BLOCK)
        p_own = p[..., n_sel:]
        return jnp.einsum('bhqjk,bhqjkd->bhqd', p_sel, vg) + jnp.einsum('bhqk,bhkd->bhqd', p_own, vo)

    o = lax.map(attend_block, jnp.arange(s_ // Q_BLOCK))
    o = o.transpose(1, 0, 3, 2, 4).reshape(b_, s_, A_HEADS * A_DH)
    return o @ w_o

def second_inputs(seed: int = 0) -> dict:
    key = jax.random.key(seed)
    ks = jax.random.split(key, 20)
    f32 = jnp.float32

    def w(k, shape, fan_in, scale=1.0):
        return jax.random.normal(k, shape, f32) * (scale * fan_in ** -0.5)

    def gain(k, shape):
        return 1.0 + 0.05 * jax.random.normal(k, shape, f32)

    res_scale = (2 * DEPTH_2) ** -0.5
    gate_base = jnp.stack([jnp.zeros((M_HEADS,), f32), jnp.linspace(3.0, 6.0, M_HEADS, dtype=f32)])
    return {
        'x': jax.random.normal(ks[0], (BATCH, SEQ, D_MODEL), f32),
        'a_norm': gain(ks[1], (N_A, D_MODEL)),
        'a_w_in': w(ks[2], (N_A, D_MODEL, M_IN), D_MODEL),
        'a_b_gates': gate_base[None] + 0.1 * jax.random.normal(ks[3], (N_A, 2, M_HEADS), f32),
        'a_h_norm': gain(ks[4], (N_A, M_HEADS * M_DV)),
        'a_w_out': w(ks[5], (N_A, D_MODEL, D_MODEL), D_MODEL, res_scale),
        'kv_norm': gain(ks[6], (D_MODEL,)),
        'w_kv': w(ks[7], (D_MODEL, 2 * D_MODEL), D_MODEL),
        'k_norm': gain(ks[8], (A_DH,)),
        'b_norm': gain(ks[9], (N_B, D_MODEL)),
        'b_w_q': w(ks[10], (N_B, D_MODEL, D_MODEL), D_MODEL),
        'b_q_norm': gain(ks[11], (N_B, A_DH)),
        'b_w_o': w(ks[12], (N_B, D_MODEL, D_MODEL), D_MODEL, res_scale),
        'f_norm': gain(ks[13], (DEPTH_2, D_MODEL)),
        'f_w_up': w(ks[14], (DEPTH_2, D_MODEL, 2 * D_FF), D_MODEL),
        'f_conv_w': w(ks[15], (DEPTH_2, CONV_W, 2 * D_FF), CONV_W),
        'f_conv_b': 0.02 * jax.random.normal(ks[16], (DEPTH_2, 2 * D_FF), f32),
        'f_w_down': w(ks[17], (DEPTH_2, D_FF, D_MODEL), D_FF, res_scale),
    }

def second_block(x, a_norm, a_w_in, a_b_gates, a_h_norm, a_w_out, kv_norm, w_kv, k_norm,
              b_norm, b_w_q, b_q_norm, b_w_o, f_norm, f_w_up, f_conv_w, f_conv_b, f_w_down):
    cos, sin = rope_tables(x.shape[1])
    h = x
    kb = vb = kmean = None
    for l in range(DEPTH_2):
        if l < N_A:
            h = h + mlstm_mixer(h, a_norm[l], a_w_in[l], a_b_gates[l], a_h_norm[l], a_w_out[l])
        else:
            j = l - N_A
            h = h + moba_mixer(h, b_norm[j], b_w_q[j], b_q_norm[j], b_w_o[j], kb, vb, kmean, cos, sin)
        h = h + conv_ffn_2(h, f_norm[l], f_w_up[l], f_conv_w[l], f_conv_b[l], f_w_down[l])
        if l == N_A - 1:
            kb, vb, kmean = shared_kv(h, kv_norm, w_kv, k_norm, cos, sin)
    return h


def setup_inputs(seed=0):
    out = dict(first_inputs(seed))
    for name, value in second_inputs(seed + 1).items():
        if name != "x":
            out[name + "_2"] = value
    return out


def reference(
    x, mem, norm1_g, w_in, shift_mu, decay_w0, decay_w2, iclr_a0, iclr_a2, gate_g2, k_k, k_a,
    r_k, lnx_g, lnx_b, vres_v0, vres_v1, vres_v2, sb_q_norm_g, sb_k_norm_g, mem_norm_g,
    w_mem_kv, mem_q_norm_g, mem_k_norm_g, w_branch, w_out, norm2_g, w_up, conv_w, conv_b,
    w_down, a_norm_2, a_w_in_2, a_b_gates_2, a_h_norm_2, a_w_out_2, kv_norm_2, w_kv_2, k_norm_2,
    b_norm_2, b_w_q_2, b_q_norm_2, b_w_o_2, f_norm_2, f_w_up_2, f_conv_w_2, f_conv_b_2,
    f_w_down_2,
):
    x = first_block(
        x, mem, norm1_g, w_in, shift_mu, decay_w0, decay_w2, iclr_a0, iclr_a2, gate_g2, k_k,
        k_a, r_k, lnx_g, lnx_b, vres_v0, vres_v1, vres_v2, sb_q_norm_g, sb_k_norm_g, mem_norm_g,
        w_mem_kv, mem_q_norm_g, mem_k_norm_g, w_branch, w_out, norm2_g, w_up, conv_w, conv_b,
        w_down,
    )
    return second_block(
        x, a_norm_2, a_w_in_2, a_b_gates_2, a_h_norm_2, a_w_out_2, kv_norm_2, w_kv_2, k_norm_2,
        b_norm_2, b_w_q_2, b_q_norm_2, b_w_o_2, f_norm_2, f_w_up_2, f_conv_w_2, f_conv_b_2,
        f_w_down_2,
    )


_drawn_inputs = setup_inputs


def setup_inputs(seed=0):
    import zlib

    import numpy as np

    out = dict(_drawn_inputs(seed))
    spreads = {}
    factors = {'decay_w2': 6.812,
     'iclr_a0': 4.123,
     'k_k': 4.18,
     'k_a': 2.86,
     'lnx_g': 3.355,
     'lnx_b': 8.0,
     'sb_q_norm_g': 6.12,
     'sb_k_norm_g': 5.764,
     'mem_norm_g': 8.0,
     'mem_q_norm_g': 8.0,
     'mem_k_norm_g': 8.0,
     'conv_b': 3.658,
     'a_h_norm_2': 5.182,
     'kv_norm_2': 8.0,
     'k_norm_2': 8.0,
     'b_norm_2': 8.0,
     'b_q_norm_2': 8.0,
     'f_conv_b_2': 6.134}
    for name, (base, spread) in spreads.items():
        noise = np.random.default_rng([zlib.crc32(name.encode()), seed]).standard_normal(out[name].shape)
        drawn = base * np.exp(spread * noise) if base else spread * noise
        out[name] = __import__('jax').numpy.asarray(drawn.astype(out[name].dtype))
    for name, factor in factors.items():
        out[name] = (out[name] * factor).astype(out[name].dtype)
    return out
```

```python
from contextlib import ExitStack

import concourse.bass as bass
from concourse import mybir
import numpy as np

F32 = mybir.dt.float32
ALU = mybir.AluOpType
ACT = mybir.ActivationFunctionType
AX = mybir.AxisListType

P = 128
T = 256
TT = T // P
D = 1024
KD = D // P
FF = 2816
KF = FF // P
W4 = 512 // P
CH = 64
NEG = -1e30
SLOT = 16
RING = 4
DECAY = float(np.exp(-0.5))

PARAMS = [("n1", 8), ("mg", 8), ("mu", 14), ("w0", 4), ("a0", 4), ("kk", 4), ("ka", 4), ("rk", 4),
          ("lg", 4), ("lb", 4), ("sbq", 1), ("sbk", 1), ("mq", 1), ("mk", 1), ("n2", 8),
          ("an", 8), ("bi", 1), ("bf", 1), ("ah", 8), ("kvn", 8), ("kn", 1), ("bn", 8), ("bq", 1),
          ("f0", 8), ("f1", 8)]
for _f in range(3):
    PARAMS += [(f"cw{_f}", 3 * 2 * KF), (f"cb{_f}", 2 * KF)]
PCOL, _at = {}, 0
for _n, _k in PARAMS:
    PCOL[_n] = _at
    _at += _k
NPAR = _at

CONSTS = [("ident", P), ("ones", P), ("bones", P), ("mask4", 4 * P), ("lev", 6 * P), ("rev", P),
          ("negS", 3 * P), ("posI", 2 * P), ("negC", 3 * P), ("cos", T), ("sin", T), ("rot", P),
          ("scan", T), ("sel", 4 * P), ("one", T), ("eps", 2)]
CCOL, _at = {}, 0
for _n, _k in CONSTS:
    CCOL[_n] = (_at, _k)
    _at += _k
NCON = _at


def constants():
    c = np.zeros((P, NCON), np.float32)

    def put(name, a):
        at, k = CCOL[name]
        c[:a.shape[0], at:at + k] = a
    i = np.arange(P)
    s, t = i[:, None], i[None, :]
    same = (s // CH) == (t // CH)
    put("ident", np.eye(P))
    put("ones", np.ones((P, P)))
    put("bones", same * 1.0)
    strict, incl = same & (s < t), same & (s <= t)
    put("mask4", np.concatenate([strict * 1.0, incl * 1.0, strict * -1.0, incl * 1.0], 1))
    lev = []
    for m in (1, 2, 4, 8, 16, 32):
        off = (s // (2 * m) == t // (2 * m)) & ((s // m) % 2 == 1) & ((t // m) % 2 == 0)
        lev.append(np.eye(P) - off)
    put("lev", np.concatenate(lev, 1))
    put("rev", (s >= t) * 1.0)
    z = np.zeros((P, P))
    put("negS", np.concatenate([(s >= t) * NEG, z, (s >= t) * NEG], 1))
    put("posI", np.concatenate([(s > t) * -NEG, z], 1))
    put("negC", np.concatenate([(t > s) * NEG, z, (t > s) * NEG], 1))
    half = 16
    inv = 500000.0 ** (-np.arange(0, 32, 2, dtype=np.float32) / np.float32(32))
    ang = np.arange(T, dtype=np.float32)[None, :] * inv.astype(np.float32)[:, None]
    cos, sin = np.ones((P, T)), np.zeros((P, T))
    cos[:half] = cos[half:2 * half] = np.cos(ang)
    sin[:half] = sin[half:2 * half] = np.sin(ang)
    put("cos", cos)
    put("sin", sin)
    rot = np.zeros((P, P))
    for m in range(half):
        rot[m + half, m] = -1.0
        rot[m, m + half] = 1.0
    put("rot", rot)
    put("scan", np.tile((np.arange(T) % CH != 0) * 1.0, (P, 1)))
    sel = np.zeros((4, 4 * P))
    for h in range(4):
        sel[h, h * P:(h + 1) * P] = 1.0
    put("sel", sel)
    put("one", np.ones((P, T)))
    put("eps", np.tile(np.array([[1e-6, 64e-5]]), (P, 1)))
    return c


def ffn_units(f):
    return [f"up{f}.{u}" for u in range(KF)] + [f"down{f}.{u}" for u in range(KD // 2)]


LIN = ([f"rw{u}" for u in range(7)] + ["sq0", "sq1", "sk0", "sk1", "sv0", "sv1", "mq0", "mq1",
       "mk0", "mk1", "mv0", "mv1"] + [f"br{m}.{n}" for m in range(KD) for n in range(3)]
       + [f"wo{u}" for u in range(4)] + ffn_units(0)
       + ["lq0", "lq1", "lk0", "lk1", "lv00", "lv01", "lv10", "lv11", "lo0", "lo1", "lo2", "lo3"]
       + [f"aw{u}" for u in range(4)] + ffn_units(1)
       + [f"bk{u}" for u in range(4)] + ["bv00", "bv01", "bv10", "bv11"]
       + [f"bq{u}" for u in range(4)] + [f"bo{u}" for u in range(4)] + ffn_units(2))
SM = (["rx", "rm", "dl0", "dl1", "al0", "al1", "gl0", "gl1", "kn0", "kn1",
       "sqn0", "sqn1", "skn0", "skn1", "mqn0", "mqn1", "mkn0", "mkn1", "bon0", "bon1"]
      + [f"z{h}" for h in range(8)] + [f"cs{h}" for h in range(8)] + [f"so{c}" for c in range(4)])
SM += ["ms0"]
for _h in range(4):
    SM += ([f"ms{_h + 1}"] if _h < 3 else []) + [f"mt{_h}", f"mo{_h}"]
SM += [f"tr{t}.{n}" for t in range(TT) for n in "vbka"]
SM += [f"qd{i}" for i in range(16)] + [f"mm{t}" for t in range(TT)]
SM += [f"l0x{g}" for g in range(4)] + [f"l0t{g}" for g in range(4)]
for _l in range(1, 6):
    SM += [f"l{_l}p{g}" for g in range(4)]
    SM += [n for g in range(4) for n in (([f"l{_l}x{g}"] if _l < 5 else []) + [f"l{_l}t{g}"])]
SM += [n for t in range(TT) for n in (f"ut{t}.0", f"ut{t}.1", f"zz{t}")]
for _q in range(4):
    SM += ([f"sa{_q}"] if _q else []) + ([f"st{_q}"] if _q < 3 else [])
SM += [f"y{c}" for c in range(4)] + ["mean0", "mean1", "var0", "var1"]
SM += ["r2", "r3", "gt", "gcol"]
for _h in range(4):
    SM += [f"mb{_h}", f"sc{_h}", f"dn{_h}", f"nm{_h}"]
SM += ["hn0", "hn1", "r4", "r5"]
for _x in "kq":
    SM += [f"b{_x}n{u}" for u in range(4)] + [f"b{_x}r{u}" for u in range(4)]
SM += ["as0"]
for _h in range(8):
    SM += ([f"as{_h + 1}"] if _h < 7 else []) + [f"at{_h}", f"ao{_h}"]
SM += ["r6"]


def program(nc, ins, out):
    ctx = ExitStack()
    with ctx:
        sems = {}

        def sem(name):
            if name not in sems:
                sems[name] = ctx.enter_context(nc.semaphore(name))
            return sems[name]

        psA = [ctx.enter_context(nc.psum_tensor(f"psA{i}", [P, 512], F32)) for i in range(4)]
        psB = [ctx.enter_context(nc.psum_tensor(f"psB{i}", [P, 512], F32)) for i in range(4)]
        unit = {n: ("A", i) for i, n in enumerate(LIN)}
        unit.update({n: ("B", i) for i, n in enumerate(SM)})
        assert len(unit) == len(LIN) + len(SM)

        def bank(name):
            r, i = unit[name]
            return (psA if r == "A" else psB)[i % 4]

        def full(name):
            r, i = unit[name]
            return sem(f"full{r}{i % 4}"), i // 4 + 1

        def free(name):
            r, i = unit[name]
            return sem(f"free{r}{i % 4}")

        def freed(name):
            return free(name), unit[name][1] // 4 + 1

        KB = 256
        arena = ctx.enter_context(nc.sbuf_tensor("arena", [P, 206 * KB], F32))

        def view(kb, c, n, off=0):
            at = int(kb * KB) + off
            v = arena[:, at:at + c * n]
            return v.rearrange("p (c n) -> p c n", c=c) if c > 1 else v

        ring = [view(8 * i, 1, SLOT * P) for i in range(RING)]
        xT = view(32, KD, T)
        hT = view(40, KD, T)
        con = view(48, 1, NCON)
        par = view(66, 1, NPAR)
        assert NCON <= 18 * KB and NPAR <= 3.5 * KB
        small = view(69.5, 1, 128)
        rstd = view(70, 1, T)
        lora = view(71, 1, 1024)
        wgate = view(75, KD, 8)
        base = 76
        pb = view(base, 14, T)
        T2 = view(base, 4, 512)
        ys = view(base + 14, 12, T)
        r0 = base + 26
        SG = view(r0, 4, T)
        LC = view(r0 + 4, 4, T)
        AA = view(r0 + 8, 4, T)
        GG = view(r0 + 12, 4, T)
        K1 = view(r0 + 16, 4, T)
        AR = view(r0 + 20, 8, T)
        KM = view(r0 + 28, 4, T)
        BN = view(r0 + 32, 4, T)
        GT = view(r0 + 36, 4, T)
        sq8 = view(r0 + 28, KD, T)
        rstdm = view(r0 + 36, 1, T)
        ST = [None, view(r0, 4, P), view(r0, 4, P, 512), view(r0 + 28, 4, P)]
        UT = view(r0 + 20, 4, T)
        ZZ = view(r0 + 16, TT, 512)
        MM = view(r0 + 4, TT, 512)
        SA = view(r0 + 8, TT, 512)
        z0 = r0 + 40
        memT = view(z0, KD, T)
        memn = view(z0 + 8, KD, T)
        mP = view(z0, 2, 512)
        mPT = view(z0 + 4, 2, 512)
        tok = view(z0, 8, 512)
        sgm = view(z0, 2, T)
        prod = view(z0 + 2, 1, T)
        mg = view(z0 + 4, KD, T)
        z1 = z0 + 16
        sbqk = view(z1, 8, T)
        sbv = view(z1 + 8, TT, 512)
        mqk = view(z1 + 12, 8, T)
        mv = view(z1 + 20, TT, 512)
        zb = view(z1 + 24, 8, 384)
        eb = view(z1 + 36, 8, 384)
        sqs = view(z1 + 24, 8, T)
        sqm = view(z1 + 36, 8, T)
        quad = view(z1, 16, 512)
        X = view(z1 + 32, 4, 512)
        XT = view(z1 + 40, 4, 512)
        YT = view(z1 + 32, 4, T)
        YQ = view(z1 + 40, 4, T)
        act_ = view(r0, KF, T)
        acc = view(r0 + 22, 2, 512)
        sil = view(r0 + 26, 2, T)
        lqk = view(base, 8, T)
        lv = view(base + 8, TT, D)
        og = view(base + 16, KD, T)
        rowLF = view(base + 24, 1, T)
        rowF = view(base + 25, 1, T)
        rowG = view(base + 26, 1, T)
        rowM2 = view(base + 27, 1, 2 * T)
        rowT = view(base + 29, 1, T)
        EM = view(base + 30, 2, T)
        ET = view(base + 32, 2, 384)
        SS = view(base + 35, 2, 384)
        dn = view(base + 38, 2, T)
        hr = view(base + 40, KD, T)
        sq2 = view(base + 48, KD, T)
        hsd = view(base + 64, 4, T)
        h2 = view(base, KD, T)
        ak = view(base + 8, KD, T)
        aq = view(base + 16, KD, T)
        av = view(base + 24, TT, D)
        ao = view(base + 32, KD, T)
        asq = view(base + 40, KD, T)
        atm = view(base + 48, KD, T)
        aS = view(base + 56, 2, 384)
        aP = view(base + 59, 2, 384)
        aPT = view(base + 62, 2, 384)

        def cst(name, rows=P):
            at, k = CCOL[name]
            return con[0:rows, at:at + k]

        def pcol(name, i=0, rows=P):
            return par[0:rows, PCOL[name] + i:PCOL[name] + i + 1]

        ident, ones, bones = cst("ident"), cst("ones"), cst("bones")
        eps6, epsln = con[:, CCOL["eps"][0]:CCOL["eps"][0] + 1], con[:, CCOL["eps"][0] + 1:CCOL["eps"][0] + 2]
        omm = small[:, 0:14]
        UPS = KF

        def bc(ap, n):
            return ap.unsqueeze(1).to_broadcast([ap.shape[0], n, ap.shape[1]])

        def ready(eng, name, n=1):
            eng.wait_ge(sem(name), n)

        def up_loop(eng, body):
            for j in range(4):
                body(0, j)
            with eng.Fori(1, UPS // 4) as i:
                for j in range(4):
                    body(i, j)
            for j in range(UPS % 4):
                body(UPS // 4, j)

        block = ctx.enter_context(nc.Block())

        @block.sync
        def _(sp):
            sp.dma_start(xT, ins["x"]).then_inc(sem("ld_x"), 16)
            sp.dma_start(con, ins["con"]).then_inc(sem("ld_con"), 16)
            nslots = ins["w"].shape[0]
            assert nslots % RING == 0

            def slot(i, j):
                sp.dma_start(ring[j], ins["w"][bass.ds(i * RING + j, 1), :, :]
                             .rearrange("a p n -> p (a n)")).then_inc(sem(f"w{j}"), 16)
            for j in range(RING):
                slot(0, j)
            with sp.Fori(1, nslots // RING) as i:
                for j in range(RING):
                    sp.wait_ge(sem("slots_used"), i * RING + (j - RING + 1))
                    slot(i, j)
            ready(sp, "x_final", 4)
            sp.dma_start(out, xT).then_inc(sem("stored"), 16)
            sp.wait_ge(sem("stored"), 16)

        @block.tensor
        def _(pe):
            state = {"slot": 0, "blk": 0, "A": 0, "B": 0, "inc": False}

            def mm(o, l, r, start, stop):
                ins_ = nc.tensor.matmul(o, l, r, start=start, stop=stop)
                if state["inc"]:
                    ins_.then_inc(sem("slots_used"), 1)
                    state["inc"] = False
                return ins_

            def weights(n):
                s, b = state["slot"], state["blk"]
                if b == 0:
                    pe.wait_ge(sem(f"w{s % RING}"), 16 * (s // RING + 1))
                    state["inc"] = s > 0
                state["blk"] = b + n
                if state["blk"] == SLOT:
                    state["slot"], state["blk"] = s + 1, 0
                return ring[s % RING][:, b * P:(b + n) * P]

            def open_(name):
                r, i = unit[name]
                assert state[r] == i, (name, i, state[r])
                state[r] += 1
                if i >= 4:
                    pe.wait_ge(free(name), i // 4)
                return bank(name)

            def close(ins_, name):
                ins_.then_inc(full(name)[0], 1)

            def project(names, rhs, wait=None, nk=KD):
                for n, name in enumerate(names):
                    o = open_(name)
                    for m in range(2):
                        for k in range(nk):
                            w = weights(1)
                            if wait and n == 0 and m == 0:
                                pe.wait_ge(sem(wait), k + 1)
                            last = mm(o[:, m * T:(m + 1) * T], w, rhs[:, k, :], k == 0, k == nk - 1)
                    close(last, name)

            def project_tok(names, src, wait=None):
                o = [open_(n) for n in names]
                for k in range(KD):
                    w = weights(4)
                    if wait:
                        pe.wait_ge(sem(wait), k + 1)
                    for t in range(TT):
                        last = mm(o[t][:, :], src[:, k, t * P:(t + 1) * P], w, k == 0, k == KD - 1)
                        if k == KD - 1:
                            close(last, names[t])

            def sum_squares(name, tag, sq):
                o = open_(name)
                ready(pe, f"sq_{tag}")
                for k in range(KD):
                    last = mm(o[:, 0:T], ones, sq[:, k, :], k == 0, k == KD - 1)
                close(last, name)

            def reduce_pairs(names, lhs, src, s, n0=0):
                for u, name in enumerate(names):
                    o = open_(name)
                    ready(pe, s, n0 + u + 1)
                    close(mm(o[:, :], lhs, src[:, 2 * u:2 * u + 2, :], True, True), name)

            pe.wait_ge(sem("ld_con"), 16)
            sum_squares("rx", "x", sq8)
            sum_squares("rm", "m", sq8)
            project([f"rw{u}" for u in range(7)], hT, "h_x")
            project(["sq0", "sq1"], hT)
            pe.wait_ge(sem("ld_lora"), 48)
            for name, lo, hi, col, ch, need in (("dl", 0, 64, 0, 12, 1), ("al", 64, 128, 0, 12, 1),
                                               ("gl", 0, 128, 512, 13, 2)):
                for u in range(2):
                    o = open_(f"{name}{u}")
                    ready(pe, "lora_in", need)
                    for m in range(2):
                        c = 2 * u + m
                        last = mm(o[:, m * T:(m + 1) * T], lora[lo:hi, col + c * P:col + (c + 1) * P],
                                  pb[lo:hi, ch, :], True, True)
                    close(last, f"{name}{u}")
            reduce_pairs(["kn0", "kn1"], bones, BN, "kk_sq")
            project(["sk0", "sk1"], hT)
            project_tok(["sv0", "sv1"], hT)
            project(["mq0", "mq1"], hT)
            project(["mk0", "mk1"], memn, "h_m")
            project_tok(["mv0", "mv1"], memn)
            reduce_pairs(["sqn0", "sqn1", "skn0", "skn1"], bones, sqs, "sb_sq")
            reduce_pairs(["mqn0", "mqn1", "mkn0", "mkn1"], ones, sqm, "mem_sq")
            reduce_pairs(["bon0", "bon1"], bones, BN, "bonus_in")
            for h in range(8):
                c, r = h // 2, 64 * (h % 2)
                o = open_(f"z{h}")
                if h == 0:
                    ready(pe, "sb_n", 4)
                mm(o[:, 0:T], sbqk[r:r + 64, 4 + c, 0:P], sbqk[r:r + 64, c, :], True, True)
                close(mm(o[:, T:T + P], sbqk[r:r + 64, 4 + c, P:T], sbqk[r:r + 64, c, P:T], True, True),
                      f"z{h}")
            for h in range(8):
                o = open_(f"cs{h}")
                ready(pe, "sb_sp", h // 4 + 1)
                mm(o[:, 0:384], cst("rev"), eb[:, h, :], True, False)
                close(mm(o[:, P:T], ones, eb[:, h, T:T + P], False, True), f"cs{h}")
            for c in range(4):
                o = open_(f"so{c}")
                ready(pe, "sb_p", c // 2 + 1)
                for hh in range(2):
                    mm(o[:, hh * T:(hh + 1) * T], sbv[:, 0, c * P:(c + 1) * P], zb[:, 2 * c + hh, 0:T],
                       True, False)
                    last = mm(o[:, hh * T + P:(hh + 1) * T], sbv[:, 1, c * P:(c + 1) * P],
                              zb[:, 2 * c + hh, T:T + P], False, True)
                close(last, f"so{c}")

            def mem_scores(h):
                o = open_(f"ms{h}")
                if h == 0:
                    ready(pe, "mem_n", 4)
                for t in range(TT):
                    last = mm(o[:, t * T:(t + 1) * T], mqk[:, h, t * P:(t + 1) * P], mqk[:, 4 + h, :],
                              True, True)
                close(last, f"ms{h}")
            mem_scores(0)
            for h in range(4):
                if h < 3:
                    mem_scores(h + 1)
                o = open_(f"mt{h}")
                ready(pe, "mem_p", h + 1)
                for m in range(2):
                    for t in range(TT):
                        last = nc.tensor.transpose(o[:, (2 * m + t) * P:(2 * m + t + 1) * P],
                                                   mP[:, h % 2, t * T + m * P:t * T + (m + 1) * P], ident)
                close(last, f"mt{h}")
                o = open_(f"mo{h}")
                pe.wait_ge(*freed(f"mt{h}"))
                for m in range(2):
                    last = mm(o[:, 0:T], mv[:, m, h * P:(h + 1) * P], mPT[:, h % 2, m * T:(m + 1) * T],
                              m == 0, m == 1)
                close(last, f"mo{h}")

            for t in range(TT):
                for n, src in (("v", pb[:, 8:12, :]), ("b", K1), ("k", LC), ("a", AR[:, 0:4, :])):
                    name = f"tr{t}.{n}"
                    o = open_(name)
                    if t == 0:
                        ready(pe, "fm", {"v": 1, "a": 1, "b": 2, "k": 3}[n])
                    for c in range(4):
                        last = nc.tensor.transpose(o[:, c * P:(c + 1) * P], src[:, c, t * P:(t + 1) * P],
                                                   ident)
                    close(last, name)
            ARv = AR.rearrange("p (a c) n -> p a c n", a=2)
            for i in range(16):
                t, h = i // 8, i % 8
                c, r = h // 2, 64 * (h % 2)
                o = open_(f"qd{i}")
                for m, src in enumerate((K1, LC)):
                    last = mm(o[:, m * T:(m + 1) * T], src[r:r + 64, c, t * P:(t + 1) * P],
                              ARv[r:r + 64, :, c, t * P:(t + 1) * P], True, True)
                close(last, f"qd{i}")
            for t in range(TT):
                o = open_(f"mm{t}")
                pe.wait_ge(*freed(f"tr{t}.v"))
                for h in range(8):
                    if h % 4 == 0:
                        pe.wait_ge(*freed(f"qd{t * 8 + h + 3}"))
                    last = mm(o[:, h * 64:(h + 1) * 64], quad[:, t * 8 + h, T:T + P],
                              tok[:, t * 4, h * 64:(h + 1) * 64], True, True)
                close(last, f"mm{t}")
            for g in range(4):
                o = open_(f"l0x{g}")
                ready(pe, "LT", g + 1)
                for i in range(4):
                    last = mm(o[:, i * P:(i + 1) * P], quad[:, 4 * g + i, 0:P], ident, True, True)
                close(last, f"l0x{g}")
            for g in range(4):
                o = open_(f"l0t{g}")
                pe.wait_ge(*freed(f"l0x{g}"))
                for i in range(4):
                    last = nc.tensor.transpose(o[:, i * P:(i + 1) * P], X[:, g, i * P:(i + 1) * P], ident)
                close(last, f"l0t{g}")
            for l in range(1, 6):
                for g in range(4):
                    o = open_(f"l{l}p{g}")
                    pe.wait_ge(*freed(f"l{l - 1}x{g}"))
                    for i in range(4):
                        last = mm(o[:, i * P:(i + 1) * P], quad[:, 4 * g + i, 0:P],
                                  X[:, g, i * P:(i + 1) * P], True, True)
                    close(last, f"l{l}p{g}")
                for g in range(4):
                    pe.wait_ge(*freed(f"l{l}p{g}"))
                    pe.wait_ge(*freed(f"l{l - 1}t{g}"))
                    if l < 5:
                        o = open_(f"l{l}x{g}")
                        for i in range(4):
                            s = slice(i * P, (i + 1) * P)
                            last = mm(o[:, s], XT[:, g, s], T2[:, g, s], True, True)
                        close(last, f"l{l}x{g}")
                    o = open_(f"l{l}t{g}")
                    for i in range(4):
                        s = slice(i * P, (i + 1) * P)
                        last = mm(o[:, s], T2[:, g, s], XT[:, g, s], True, True)
                    close(last, f"l{l}t{g}")

            def XTt(i):
                return XT[:, i // 4, (i % 4) * P:(i % 4 + 1) * P]
            for t in range(TT):
                for cp in range(2):
                    o = open_(f"ut{t}.{cp}")
                    pe.wait_ge(*freed(f"l5t{2 * t + cp}"))
                    pe.wait_ge(*freed(f"tr{t}.a"))
                    for j in range(4):
                        last = mm(o[:, j * P:(j + 1) * P],
                                  tok[:, t * 4 + 3, (2 * cp + j // 2) * P:(2 * cp + j // 2 + 1) * P],
                                  XTt(t * 8 + 4 * cp + j), True, True)
                    close(last, f"ut{t}.{cp}")
                o = open_(f"zz{t}")
                pe.wait_ge(*freed(f"mm{t}"))
                for h in range(8):
                    last = mm(o[:, h * 64:(h + 1) * 64], XTt(t * 8 + h), MM[:, t, h * 64:(h + 1) * 64],
                              True, True)
                close(last, f"zz{t}")
            for q in range(4):
                t, hs = q // 2, slice(CH * (q % 2), CH * (q % 2) + CH)
                if q:
                    o = open_(f"sa{q}")
                    pe.wait_ge(*freed(f"ut{t}.0"))
                    pe.wait_ge(*freed(f"ut{t}.1"))
                    ready(pe, "state", q)
                    for c in range(4):
                        last = mm(o[:, c * P:(c + 1) * P], UT[:, c, t * P:(t + 1) * P], ST[q][:, c, :],
                                  True, True)
                    close(last, f"sa{q}")
                if q < 3:
                    o = open_(f"st{q}")
                    if q:
                        pe.wait_ge(*freed(f"sa{q}"))
                    else:
                        ready(pe, "SA0")
                    for c in range(4):
                        s = slice(c * P, (c + 1) * P)
                        mm(o[:, s], tok[hs, t * 4 + 1, s], SA[hs, t, s], True, False)
                        last = mm(o[:, s], tok[hs, t * 4 + 2, s], tok[hs, t * 4, s], False, True)
                    close(last, f"st{q}")
            pe.wait_ge(*freed("sa3"))
            for c in range(4):
                o = open_(f"y{c}")
                cs = slice(c * P, (c + 1) * P)
                for hh in range(2):
                    for t in range(TT):
                        i = t * 8 + 2 * c + hh
                        s = slice(hh * T + t * P, hh * T + (t + 1) * P)
                        mm(o[:, s], SA[:, t, cs], quad[:, i, P:T], True, False)
                        mm(o[:, s], tok[:, t * 4, cs], quad[:, i, 3 * P:4 * P], False, False)
                        for q in range(max(2 * t, 1), 2 * t + 2):
                            last = mm(o[:, hh * T + q * CH:hh * T + (q + 1) * CH], ST[q][:, c, :],
                                      AR[:, 4 + c, q * CH:(q + 1) * CH], False, q == 2 * t + 1)
                close(last, f"y{c}")
            for u in range(2):
                o = open_(f"mean{u}")
                pe.wait_ge(*freed(f"y{2 * u + 1}"))
                close(mm(o[:, :], bones, YT[:, 2 * u:2 * u + 2, :], True, True), f"mean{u}")
            reduce_pairs(["var0", "var1"], bones, YQ, "y_sq")
            ready(pe, "ys", 1)
            pe.wait_ge(*freed("so3"))
            pe.wait_ge(*freed("mo3"))
            for m in range(KD):
                for n in range(3):
                    name = f"br{m}.{n}"
                    o = open_(name)
                    for k in range(KD):
                        mm(o[:, 0:T], weights(1), hT[:, k, :], k == 0, k == KD - 1)
                    for k in range(W4):
                        last = mm(o[:, T:2 * T], weights(1), ys[:, n * W4 + k, :], k == 0, k == W4 - 1)
                    close(last, name)
            ready(pe, "merged", KD)
            project([f"wo{u}" for u in range(4)], mg)

            def ffn(f, rms):
                sum_squares(rms, f"f{f}", sq8)
                a0, s0 = unit[f"up{f}.0"][1], state["slot"]
                assert state["blk"] == 0 and state["A"] == a0

                def up(i, j):
                    ai, s = a0 + j, s0 + j
                    pe.wait_ge(sem(f"w{s % RING}"), (i + (s // RING + 1)) * 16)
                    pe.wait_ge(sem(f"freeA{ai % 4}"), i + ai // 4)
                    state["inc"] = True
                    for m in range(2):
                        for k in range(KD):
                            if isinstance(i, int) and i == 0 and j == 0 and m == 0:
                                ready(pe, f"h_f{f}", k + 1)
                            last = mm(psA[ai % 4][:, m * T:(m + 1) * T],
                                      ring[s % RING][:, (m * KD + k) * P:(m * KD + k + 1) * P],
                                      hT[:, k, :], k == 0, k == KD - 1)
                    last.then_inc(sem(f"fullA{ai % 4}"), 1)
                up_loop(pe, up)
                state["slot"], state["A"] = s0 + UPS, a0 + UPS
                for u in range(KD // 2):
                    name = f"down{f}.{u}"
                    o = open_(name)
                    for m in range(2):
                        for k in range(KF):
                            w = weights(1)
                            if u == 0 and m == 0:
                                ready(pe, "act_ready", f * UPS + k + 1)
                            last = mm(o[:, m * T:(m + 1) * T], w, act_[:, k, :], k == 0, k == KF - 1)
                    close(last, name)
            ffn(0, "r2")

            sum_squares("r3", "l", sq8)
            project(["lq0", "lq1", "lk0", "lk1"], hT, "h_l")
            project_tok(["lv00", "lv01"], hT)
            project_tok(["lv10", "lv11"], hT)
            o = open_("gt")
            pe.wait_ge(sem("ld_wg"), 16)
            for n in range(2):
                for k in range(KD):
                    last = mm(o[0:4, n * T:(n + 1) * T], wgate[:, k, 4 * n:4 * n + 4], hT[:, k, :],
                              k == 0, k == KD - 1)
            close(last, "gt")
            project([f"lo{u}" for u in range(4)], hT)
            o = open_("gcol")
            ready(pe, "g_row")
            for t in range(TT):
                last = mm(o[:, t * 4:t * 4 + 4], rowG[0:4, t * P:(t + 1) * P], ident[0:4, 0:4], True, True)
            close(last, "gcol")
            for h in range(4):
                o = open_(f"mb{h}")
                if h == 0:
                    ready(pe, "m_row")
                close(mm(o[:, :], cst("sel", 4)[:, h * P:(h + 1) * P], rowM2[0:4, :], True, True), f"mb{h}")
                o = open_(f"sc{h}")
                if h == 0:
                    pe.wait_ge(*freed("lk1"))
                mm(o[:, 0:T], lqk[:, 4 + h, 0:P], lqk[:, h, :], True, True)
                close(mm(o[:, T:T + P], lqk[:, 4 + h, P:T], lqk[:, h, P:T], True, True), f"sc{h}")
                o = open_(f"dn{h}")
                pe.wait_ge(*freed(f"sc{h}"))
                s_ = SS[:, h % 2, :]
                mm(o[:, 0:T], ones, s_[:, 0:T], True, False)
                close(mm(o[:, P:T], ones, s_[:, T:T + P], False, True), f"dn{h}")
                o = open_(f"nm{h}")
                if h == 0:
                    pe.wait_ge(*freed("lv11"))
                for e in range(2):
                    es = slice((2 * h + e) * P, (2 * h + e + 1) * P)
                    mm(o[:, e * T:(e + 1) * T], lv[:, 0, es], s_[:, 0:T], True, False)
                    last = mm(o[:, e * T + P:(e + 1) * T], lv[:, 1, es], s_[:, T:T + P], False, True)
                close(last, f"nm{h}")
            for u in range(2):
                o = open_(f"hn{u}")
                ready(pe, "l_sq", u + 1)
                for m in range(2):
                    for e in range(2):
                        last = mm(o[:, m * T:(m + 1) * T], ones, sq2[:, 4 * u + 2 * m + e, :], e == 0, e == 1)
                close(last, f"hn{u}")
            ready(pe, "l_h", KD)
            project([f"aw{u}" for u in range(4)], hr)
            ffn(1, "r4")

            sum_squares("r5", "a", sq8)
            project([f"bk{u}" for u in range(4)], hT, "h_a")
            reduce_pairs([f"bkn{u}" for u in range(4)], ones, asq, "a_sq")
            for u in range(4):
                o = open_(f"bkr{u}")
                ready(pe, "a_n", u + 1)
                close(mm(o[:, :], cst("rot"), ak[:, 2 * u:2 * u + 2, :], True, True), f"bkr{u}")
            project_tok(["bv00", "bv01"], hT)
            project_tok(["bv10", "bv11"], hT)
            ready(pe, "h_b", KD)
            project([f"bq{u}" for u in range(4)], h2)
            reduce_pairs([f"bqn{u}" for u in range(4)], ones, asq, "a_sq", 4)
            for u in range(4):
                o = open_(f"bqr{u}")
                ready(pe, "a_n", u + 5)
                close(mm(o[:, :], cst("rot"), aq[:, 2 * u:2 * u + 2, :], True, True), f"bqr{u}")

            def scores(h):
                o = open_(f"as{h}")
                ready(pe, "a_rope", 4 + h // 2 + 1)
                mm(o[:, 0:P], aq[:, h, 0:P], ak[:, h, 0:P], True, True)
                close(mm(o[:, P:3 * P], aq[:, h, P:T], ak[:, h, :], True, True), f"as{h}")
            scores(0)
            for h in range(8):
                if h < 7:
                    scores(h + 1)
                o = open_(f"at{h}")
                ready(pe, "a_p", h + 1)
                for b, s in enumerate((0, 1, 2)):
                    last = nc.tensor.transpose(o[:, b * P:(b + 1) * P], aP[:, h % 2, s * P:(s + 1) * P], ident)
                close(last, f"at{h}")
                o = open_(f"ao{h}")
                pe.wait_ge(*freed(f"at{h}"))
                if h == 0:
                    pe.wait_ge(*freed("bv11"))
                hs = slice(h * P, (h + 1) * P)
                mm(o[:, 0:T], av[:, 0, hs], aPT[:, h % 2, 0:T], True, False)
                close(mm(o[:, P:T], av[:, 1, hs], aPT[:, h % 2, T:T + P], False, True), f"ao{h}")
            pe.wait_ge(*freed("ao7"))
            project([f"bo{u}" for u in range(4)], ao)
            ffn(2, "r6")
            assert state["A"] == len(LIN) and state["B"] == len(SM)
            assert state["slot"] == ins["w"].shape[0] and state["blk"] == 0

        @block.scalar
        def _(act):
            own = [0]

            def step(ins_):
                own[0] += 1
                ins_.then_inc(sem("act_step"), 1)
                act.wait_ge(sem("act_step"), own[0])

            def take(name):
                act.wait_ge(*full(name))
                return bank(name)

            def release(ins_, name):
                ins_.then_inc(free(name), 1)

            def A(o, i, f, **kw):
                return nc.scalar.activation(o, i, f, **kw)

            def rms(tag, name, src, sq, sd):
                A(sq, src, ACT.Square).then_inc(sem(f"sq_{tag}"), 1)
                o = take(name)
                release(A(sd, o[:, 0:T], ACT.Sqrt, bias=eps6, scale=1.0 / D), name)

            act.dma_start(memT, ins["mem"]).then_inc(sem("ld_mem"), 16)
            act.dma_start(par, ins["par"]).then_inc(sem("ld_par"), 16)
            act.dma_start(lora[0:64, 0:512], ins["decay_w2"]).then_inc(sem("ld_lora"), 16)
            act.dma_start(lora[64:128, 0:512], ins["iclr_a2"]).then_inc(sem("ld_lora"), 16)
            act.dma_start(lora[:, 512:1024], ins["gate_g2"]).then_inc(sem("ld_lora"), 16)
            act.dma_start(wgate, ins["wg"]).then_inc(sem("ld_wg"), 16)
            act.wait_ge(sem("ld_x"), 16)
            act.wait_ge(sem("ld_con"), 16)
            rms("x", "rx", xT, sq8, rstd)
            act.wait_ge(sem("ld_mem"), 16)
            rms("m", "rm", memT, sq8, rstdm)
            act.wait_ge(sem("ld_par"), 16)
            ready(act, "omm")
            for u in range(7):
                o = take(f"rw{u}")
                for m in range(2):
                    c = 2 * u + m
                    A(pb[:, c, :], o[:, m * T:(m + 1) * T], ACT.Copy, scale=omm[:, c:c + 1])\
                        .then_inc(sem("shift1"), 1)

            def copy2(name, dst):
                release(A(dst, take(name)[:, :], ACT.Copy), name)
            copy2("sq0", sbqk[:, 0:2, :])
            copy2("sq1", sbqk[:, 2:4, :])
            act.wait_ge(*freed("rw6"))
            A(pb[0:64, 12, :], pb[0:64, 12, :], ACT.Tanh).then_inc(sem("lora_in"), 1)
            A(pb[:, 13, :], pb[:, 13, :], ACT.Sigmoid).then_inc(sem("lora_in"), 1)
            for name, dst, b in (("dl", SG, "w0"), ("al", AA, "a0")):
                for u in range(2):
                    o = take(f"{name}{u}")
                    for m in range(2):
                        c = 2 * u + m
                        last = A(dst[:, c, :], o[:, m * T:(m + 1) * T], ACT.Sigmoid, bias=pcol(b, c))
                        if m == 0:
                            last.then_inc(sem("act_aux"), 1)
                    release(last, f"{name}{u}")
            copy2("gl0", GT[:, 0:2, :])
            copy2("gl1", GT[:, 2:4, :])
            for u in range(2):
                release(A(KM[:, 2 * u:2 * u + 2, :], take(f"kn{u}")[:, :], ACT.Sqrt), f"kn{u}")
            copy2("sk0", sbqk[:, 4:6, :])
            copy2("sk1", sbqk[:, 6:8, :])
            ready(act, "cum", 4)
            step(A(GG, LC, ACT.Exp, scale=-DECAY))
            ready(act, "cum_prev")
            A(LC, LC, ACT.Exp, scale=DECAY).then_inc(sem("decays"), 1)
            A(SG, SG, ACT.Exp, scale=-DECAY).then_inc(sem("decays"), 1)
            copy2("sv0", sbv[:, 0, :])
            copy2("sv1", sbv[:, 1, :])
            copy2("mq0", mqk[:, 0:2, :])
            copy2("mq1", mqk[:, 2:4, :])
            copy2("mk0", mqk[:, 4:6, :])
            copy2("mk1", mqk[:, 6:8, :])
            copy2("mv0", mv[:, 0, :])
            copy2("mv1", mv[:, 1, :])
            for u, n in enumerate(("sqn0", "sqn1", "skn0", "skn1")):
                release(A(sqs[:, 2 * u:2 * u + 2, :], take(n)[:, :], ACT.Sqrt, bias=eps6, scale=1.0 / 64), n)
            for u, n in enumerate(("mqn0", "mqn1", "mkn0", "mkn1")):
                release(A(sqm[:, 2 * u:2 * u + 2, :], take(n)[:, :], ACT.Sqrt, bias=eps6, scale=1.0 / P), n)
            for f in range(2):
                hs = slice(4 * f, 4 * f + 4)
                act.wait_ge(*freed(f"z{4 * f + 3}"))
                ready(act, "mem_n", 4)
                step(A(eb[:, hs, :], zb[:, hs, :], ACT.Abs))
                step(A(eb[:, hs, :], eb[:, hs, :], ACT.Exp, scale=-1.0))
                A(eb[:, hs, :], eb[:, hs, :], ACT.Ln, bias=1.0).then_inc(sem("sb_ln"), 1)
            for f in range(2):
                act.wait_ge(*freed(f"cs{4 * f + 3}"))
                A(zb[:, 4 * f:4 * f + 4, :], zb[:, 4 * f:4 * f + 4, :], ACT.Exp).then_inc(sem("sb_p"), 1)
            for c in range(4):
                o = take(f"so{c}")
                A(ys[0:64, 4 + c, :], o[0:64, 0:T], ACT.Copy).then_inc(sem("act_aux"), 1)
                release(A(ys[64:128, 4 + c, :], o[64:128, T:2 * T], ACT.Copy), f"so{c}")

            def mem_exp(h):
                ready(act, "mem_max", h + 1)
                o = take(f"ms{h}")
                for t in range(TT):
                    last = A(mP[:, h % 2, t * T:(t + 1) * T], o[:, t * T:(t + 1) * T], ACT.Exp,
                             bias=small[:, 24 + 2 * h + t:25 + 2 * h + t], scale=P ** -0.5,
                             accum_out=small[:, 32 + 2 * h + t:33 + 2 * h + t])
                    if t == 0:
                        last.then_inc(sem("act_aux"), 1)
                release(last, f"ms{h}")
            mem_exp(0)
            for h in range(4):
                if h < 3:
                    mem_exp(h + 1)
                copy2(f"mt{h}", mPT[:, h % 2, :])
                release(A(ys[:, 8 + h, :], take(f"mo{h}")[:, 0:T], ACT.Copy), f"mo{h}")
            for t in range(TT):
                for n, name in enumerate("vbka"):
                    name = f"tr{t}.{name}"
                    release(A(tok[:, 4 * t + n, :], take(name)[:, :], ACT.Copy,
                              scale=-1.0 if n == 3 else 1.0), name)
            for t in range(TT):
                copy2(f"mm{t}", MM[:, t, :])
            for g in range(4):
                copy2(f"l0t{g}", XT[:, g, :])
            for l in range(1, 6):
                for g in range(4):
                    copy2(f"l{l}t{g}", XT[:, g, :])
            for t in range(TT):
                copy2(f"zz{t}", ZZ[:, t, :])
            for c in range(4):
                o = take(f"y{c}")
                A(YT[0:64, c, :], o[0:64, 0:T], ACT.Copy).then_inc(sem("act_aux"), 1)
                release(A(YT[64:128, c, :], o[64:128, T:2 * T], ACT.Copy), f"y{c}")
            for u in range(2):
                release(A(YQ[:, 2 * u:2 * u + 2, :], take(f"var{u}")[:, :], ACT.Sqrt, bias=epsln,
                          scale=1.0 / 64), f"var{u}")
            for i in range(KD * 3):
                name = f"br{i // 3}.{i % 3}"
                if i >= 2:
                    act.wait_ge(*freed(f"br{(i - 2) // 3}.{(i - 2) % 3}"))
                A(sgm[:, i % 2, :], take(name)[:, 0:T], ACT.Sigmoid).then_inc(sem("gate"), 1)

            def ffn(f, rms_, xready):
                ready(act, "x_final" if xready is None else xready, 4)
                rms(f"f{f}", rms_, xT, sq8, rstd)
                a0 = unit[f"up{f}.0"][1]

                def up(i, j):
                    ai = a0 + j
                    u = i * 4 + j
                    act.wait_ge(sem(f"fullA{ai % 4}"), i + ai // 4 + 1)
                    if not (isinstance(i, int) and i == 0 and j < 2):
                        ready(act, "act_ready", u + (f * UPS - 1))
                    for m in range(2):
                        cc = u * 2 + (PCOL[f"cw{f}"] + 4 * KF + m)
                        cb = u * 2 + (PCOL[f"cb{f}"] + m)
                        A(acc[:, j % 2, m * T:(m + 1) * T], psA[ai % 4][:, m * T:(m + 1) * T], ACT.Identity,
                          scale=par[:, bass.ds(cc, 1)], bias=par[:, bass.ds(cb, 1)])\
                            .then_inc(sem("tap2"), 1)
                    ready(act, "conv", u + (f * UPS + 1))
                    A(sil[:, j % 2, :], acc[:, j % 2, 0:T], ACT.Silu).then_inc(sem("silu"), 1)
                up_loop(act, up)
            ffn(0, "r2", "x1")

            ready(act, "x2", 4)
            rms("l", "r3", xT, sq8, rstd)
            for n, name in enumerate(("lq0", "lq1")):
                release(A(lqk[:, 2 * n:2 * n + 2, :], take(name)[:, :], ACT.Copy, scale=P ** -0.5), name)
            copy2("lk0", lqk[:, 4:6, :])
            copy2("lk1", lqk[:, 6:8, :])
            for a in range(2):
                for t in range(TT):
                    copy2(f"lv{a}{t}", lv[:, t, a * 512:(a + 1) * 512])
            ready(act, "f_row")
            step(A(rowT[0:4, :], rowLF[0:4, :], ACT.Abs))
            step(A(rowT[0:4, :], rowT[0:4, :], ACT.Exp, scale=-1.0))
            A(rowT[0:4, :], rowT[0:4, :], ACT.Ln, bias=1.0).then_inc(sem("f_ln"), 1)
            for u in range(4):
                release(A(og[:, 2 * u:2 * u + 2, :], take(f"lo{u}")[:, :], ACT.Sigmoid), f"lo{u}")
            step(A(small[:, 88:96], take("gcol")[:, 0:8], ACT.Copy))
            A(small[:, 96:97], small[:, 88:89], ACT.Copy).then_inc(free("gcol"), 1)
            for h in range(4):
                ready(act, "e_in", h + 1)
                step(A(ET[:, h % 2, 0:T], ET[:, h % 2, 0:T], ACT.Exp, scale=-1.0, bias=small[:, 88 + h:89 + h]))
                A(ET[:, h % 2, T:T + P], ET[:, h % 2, T:T + P], ACT.Exp, scale=-1.0,
                  bias=small[:, 92 + h:93 + h]).then_inc(sem("e_out"), 1)
                if h >= 2:
                    ready(act, "l_den", h - 1)
                release(A(EM[:, h % 2, :], take(f"mb{h}")[:, T:2 * T], ACT.Exp, scale=-1.0), f"mb{h}")
                A(dn[:, h % 2, :], take(f"dn{h}")[:, 0:T], ACT.Abs).then_inc(free(f"dn{h}"), 1)
            for u in range(2):
                release(A(hsd[:, 2 * u:2 * u + 2, :], take(f"hn{u}")[:, :], ACT.Sqrt, bias=eps6,
                          scale=1.0 / T), f"hn{u}")
            ffn(1, "r4", "x3")

            ready(act, "x4", 4)
            rms("a", "r5", xT, sq8, rstd)
            for x, dst, n0 in (("k", ak, 0), ("q", aq, 4)):
                for u in range(4):
                    copy2(f"b{x}{u}", dst[:, 2 * u:2 * u + 2, :])
                for u in range(4):
                    name = f"b{x}n{u}"
                    release(A(asq[:, 2 * u:2 * u + 2, :], take(name)[:, :], ACT.Sqrt, bias=eps6,
                              scale=1.0 / P), name)
                if x == "k":
                    for a in range(2):
                        for t in range(TT):
                            copy2(f"bv{a}{t}", av[:, t, a * 512:(a + 1) * 512])

            def a_exp(h):
                ready(act, "a_max", h + 1)
                if h >= 2:
                    act.wait_ge(*freed(f"at{h - 2}"))
                for t in range(TT):
                    s = slice(t * P, 3 * P if t else P)
                    last = A(aP[:, h % 2, s], aS[:, h % 2, s], ACT.Exp,
                             bias=small[:, 56 + 2 * h + t:57 + 2 * h + t], scale=P ** -0.5,
                             accum_out=small[:, 72 + 2 * h + t:73 + 2 * h + t])
                    last.then_inc(sem("a_e"), 1)
            a_exp(0)
            for h in range(8):
                if h < 7:
                    a_exp(h + 1)
                release(A(aPT[:, h % 2, :], take(f"at{h}")[:, 0:384], ACT.Copy), f"at{h}")
                release(A(ao[:, h, :], take(f"ao{h}")[:, 0:T], ACT.Copy), f"ao{h}")
            ffn(2, "r6", "x5")

        @block.gpsimd
        def _(pool):
            def mul(o, a, b):
                return nc.gpsimd.tensor_tensor(o, a, b, ALU.mult)
            ready(pool, "kk_in", 4)
            for u in range(2):
                s = slice(2 * u, 2 * u + 2)
                mul(BN[:, s, :], K1[:, s, :], K1[:, s, :]).then_inc(sem("kk_sq"), 1)
            ready(pool, "cum", 4)
            pool.wait_ge(*freed("dl1"))
            nc.gpsimd.tensor_tensor(SG, LC, SG, ALU.subtract).then_inc(sem("cum_prev"), 1)
            for n, (src, dst, names, s) in enumerate(((sbqk, sqs, ("sq0", "sq1", "sk0", "sk1"), "sb_sq"),
                                                      (mqk, sqm, ("mq0", "mq1", "mk0", "mk1"), "mem_sq"))):
                for u, name in enumerate(names):
                    pool.wait_ge(*freed(name))
                    c = slice(2 * u, 2 * u + 2)
                    mul(dst[:, c, :], src[:, c, :], src[:, c, :]).then_inc(sem(s), 1)
            ready(pool, "fm", 3)
            nc.gpsimd.memset(SG, 0.0).then_inc(sem("zeros"), 1)
            nc.gpsimd.memset(view(r0 + 28, 1, 512), 0.0).then_inc(sem("zeros"), 1)
            for g in range(4):
                pool.wait_ge(*freed(f"qd{4 * g + 3}"))
                v = quad[:, 4 * g:4 * g + 4, 0:P]
                nc.gpsimd.tensor_tensor(v, v, bc(ident, 4), ALU.add).then_inc(sem("LT"), 1)
            for u in range(2):
                s = slice(2 * u, 2 * u + 2)
                pool.wait_ge(*freed(f"mean{u}"))
                mul(YQ[:, s, :], YT[:, s, :], YT[:, s, :]).then_inc(sem("y_sq"), 1)

            def ffn(f):
                def up(i, j):
                    u = i * 4 + j
                    ready(pool, "silu", u + (f * UPS + 1))
                    mul(act_[:, bass.ds(u, 1), :].rearrange("p a n -> p (a n)"), sil[:, j % 2, :],
                        acc[:, j % 2, T:2 * T]).then_inc(sem("act_ready"), 1)
                up_loop(pool, up)
            ffn(0)
            for u in range(2):
                ready(pool, "l_hr", 4 * u + 4)
                s = slice(4 * u, 4 * u + 4)
                mul(sq2[:, s, :], hr[:, s, :], hr[:, s, :]).then_inc(sem("l_sq"), 1)
            ffn(1)
            for x, src, n0 in (("k", ak, 0), ("q", aq, 4)):
                for u in range(4):
                    pool.wait_ge(*freed(f"b{x}{u}"))
                    if x == "q":
                        ready(pool, "a_n", 4)
                    s = slice(2 * u, 2 * u + 2)
                    mul(asq[:, s, :], src[:, s, :], src[:, s, :]).then_inc(sem("a_sq"), 1)
                for u in range(4):
                    ready(pool, "a_n", n0 + u + 1)
                    s = slice(2 * u, 2 * u + 2)
                    mul(atm[:, s, :], src[:, s, :], bc(cst("cos"), 2)).then_inc(sem("a_cos"), 1)
                if x == "k":
                    ready(pool, "a_rope", 4)
            ffn(2)

        @block.vector
        def _(dve):
            own = [0]

            def mark(ins_):
                own[0] += 1
                ins_.then_inc(sem("dve_step"), 1)

            def settle():
                dve.wait_ge(sem("dve_step"), own[0])

            def step(ins_):
                mark(ins_)
                settle()

            def take(name):
                dve.wait_ge(*full(name))
                return bank(name)

            def release(ins_, name):
                ins_.then_inc(free(name), 1)

            V = nc.vector

            def tt(o, a, b, op):
                return V.tensor_tensor(o, a, b, op)

            def stt(o, a, s, b, op0, op1):
                return V.scalar_tensor_tensor(out=o, in0=a, scalar=s, in1=b, op0=op0, op1=op1)

            def norm(tag, name, src, dst, g, sd):
                dve.wait_ge(*freed(name))
                step(V.reciprocal(sd, sd))
                for k in range(KD):
                    stt(dst[:, k, :], src[:, k, :], pcol(g, k), sd, ALU.mult, ALU.mult)\
                        .then_inc(sem(f"h_{tag}"), 1)

            dve.wait_ge(sem("ld_par"), 16)
            V.tensor_scalar(omm, par[:, PCOL["mu"]:PCOL["mu"] + 14], -1.0, 1.0, ALU.mult, ALU.add)\
                .then_inc(sem("omm"), 1)
            dve.wait_ge(sem("ld_x"), 16)
            dve.wait_ge(sem("ld_con"), 16)
            norm("x", "rx", xT, hT, "n1", rstd)
            dve.wait_ge(sem("ld_mem"), 16)
            norm("m", "rm", memT, memn, "mg", rstdm)
            for u in range(7):
                o = take(f"rw{u}")
                for m in range(2):
                    c = 2 * u + m
                    ready(dve, "shift1", 2 * u + 2)
                    last = stt(pb[:, c, 1:T], o[:, m * T:(m + 1) * T - 1], pcol("mu", c), pb[:, c, 1:T],
                               ALU.mult, ALU.add)
                    if m == 0:
                        mark(last)
                release(last, f"rw{u}")
            settle()
            dve.wait_ge(*freed("rw6"))
            r_, k_, v_ = pb[:, 0:4, :], pb[:, 4:8, :], pb[:, 8:12, :]
            for c in range(4):
                V.tensor_scalar(K1[:, c, :], k_[:, c, :], pcol("kk", c), None, ALU.mult)\
                    .then_inc(sem("kk_in"), 1)
            dve.wait_ge(*freed("dl1"))
            for c in range(4):
                V.tensor_tensor_scan(LC[:, c, :], cst("scan"), SG[:, c, :], 0.0, ALU.mult, ALU.add)\
                    .then_inc(sem("cum"), 1)
            for u in range(2):
                dve.wait_ge(*freed(f"kn{u}"))
            step(V.tensor_scalar(KM, KM, 1e-12, None, ALU.max))
            step(V.reciprocal(KM, KM))
            step(tt(K1, K1, KM, ALU.mult))
            dve.wait_ge(*freed("al1"))
            ready(dve, "decays", 2)
            mark(tt(AR[:, 0:4, :], K1, SG, ALU.mult))
            settle()
            mark(tt(K1, K1, AA, ALU.mult))
            tt(AR[:, 4:8, :], r_, GG, ALU.mult).then_inc(sem("fm"), 1)
            settle()
            tt(K1, K1, LC, ALU.mult).then_inc(sem("fm"), 1)
            for c in range(4):
                mark(V.tensor_scalar(AA[:, c, :], AA[:, c, :], -1.0, pcol("ka", c), ALU.add, ALU.mult))
            settle()
            step(stt(KM, AA, 1.0, k_, ALU.add, ALU.mult))
            for c in range(4):
                mark(stt(BN[:, c, :], r_[:, c, :], pcol("rk", c), KM[:, c, :], ALU.mult, ALU.mult))
            settle()
            tt(LC, KM, LC, ALU.mult).then_inc(sem("fm"), 1)
            V.memset(small[:, 120:121], 0.0).then_inc(sem("bonus_in"), 1)
            V.memset(small[:, 121:122], 0.0).then_inc(sem("bonus_in"), 1)

            def head_norm(sq, dst, names, g, s, width=512):
                for u, name in enumerate(names):
                    c = slice(2 * u, 2 * u + 2)
                    dve.wait_ge(*freed(name))
                    step(V.reciprocal(sq[:, c, :], sq[:, c, :]))
                    stt(dst[:, c, :], dst[:, c, :], g[u], sq[:, c, :], ALU.mult, ALU.mult)\
                        .then_inc(sem(s), 1)
            head_norm(sqs, sbqk, ("sqn0", "sqn1", "skn0", "skn1"), [pcol("sbq")] * 2 + [pcol("sbk")] * 2, "sb_n")
            head_norm(sqm, mqk, ("mqn0", "mqn1", "mkn0", "mkn1"), [pcol("mq")] * 2 + [pcol("mk")] * 2, "mem_n")
            for u in range(2):
                c = slice(2 * u, 2 * u + 2)
                release(tt(BN[:, c, :], take(f"bon{u}").rearrange("p (c n) -> p c n", c=2), v_[:, c, :],
                           ALU.mult), f"bon{u}")
            ready(dve, "sb_n", 4)
            for h in range(8):
                release(stt(zb[:, h, :], take(f"z{h}")[:, 0:384], 0.125, cst("negS"), ALU.mult, ALU.add),
                        f"z{h}")
            for f in range(2):
                hs = slice(4 * f, 4 * f + 4)
                ready(dve, "sb_ln", f + 1)
                dve.wait_ge(*freed(f"z{4 * f + 3}"))
                stt(eb[:, hs, :], zb[:, hs, :], 0.0, eb[:, hs, :], ALU.max, ALU.add).then_inc(sem("sb_sp"), 1)
            for h in range(8):
                release(tt(zb[:, h, :], zb[:, h, :], take(f"cs{h}")[:, 0:384], ALU.subtract), f"cs{h}")

            def mem_max(h):
                o = take(f"ms{h}")
                mx = small[:, 16 + 2 * h:18 + 2 * h]
                step(V.tensor_reduce(mx, o.rearrange("p (t n) -> p t n", t=2), AX.X, ALU.max))
                V.tensor_scalar(small[:, 24 + 2 * h:26 + 2 * h], mx, -P ** -0.5, None, ALU.mult)\
                    .then_inc(sem("mem_max"), 1)
            mem_max(0)
            for h in range(4):
                if h < 3:
                    mem_max(h + 1)
                dve.wait_ge(*freed(f"ms{h}"))
                rs = small[:, 32 + 2 * h:34 + 2 * h]
                step(V.reciprocal(rs, rs))
                mark(V.tensor_scalar(mP[:, h % 2, 0:T], mP[:, h % 2, 0:T], rs[:, 0:1], None, ALU.mult))
                settle()
                V.tensor_scalar(mP[:, h % 2, T:2 * T], mP[:, h % 2, T:2 * T], rs[:, 1:2], None, ALU.mult)\
                    .then_inc(sem("mem_p"), 1)
            for i in range(16):
                release(tt(quad[:, i, :], take(f"qd{i}")[:, :], cst("mask4"), ALU.mult), f"qd{i}")

            def lev(l):
                at = CCOL["lev"][0] + l * P
                return bc(con[:, at:at + P], 4)

            def four(ap):
                return ap.rearrange("p (i n) -> p i n", i=4)
            for g in range(4):
                release(tt(four(X[:, g, :]), four(take(f"l0x{g}")[:, :]), lev(0), ALU.mult), f"l0x{g}")
            for l in range(1, 6):
                for g in range(4):
                    release(tt(four(T2[:, g, :]), four(take(f"l{l}p{g}")[:, :]), lev(l), ALU.mult),
                            f"l{l}p{g}")
                if l < 5:
                    for g in range(4):
                        release(V.tensor_copy(X[:, g, :], take(f"l{l}x{g}")[:, :]), f"l{l}x{g}")
            for t in range(TT):
                for cp in range(2):
                    name = f"ut{t}.{cp}"
                    o = take(name).rearrange("p (c h n) -> p c h n", c=2, h=2)
                    d = UT[:, 2 * cp:2 * cp + 2, t * P:(t + 1) * P]
                    mark(V.tensor_copy(d[0:64], o[0:64, :, 0, :]))
                    settle()
                    release(V.tensor_copy(d[64:128], o[64:128, :, 1, :]), name)
            ready(dve, "zeros", 2)
            for q in range(4):
                t, hs = q // 2, slice(CH * (q % 2), CH * (q % 2) + CH)
                if q == 0:
                    dve.wait_ge(*freed("zz0"))
                    V.tensor_copy(SA[hs, 0, :], ZZ[hs, 0, :]).then_inc(sem("SA0"), 1)
                else:
                    dve.wait_ge(*freed(f"zz{t}"))
                    release(tt(SA[hs, t, :], take(f"sa{q}")[hs, :], ZZ[hs, t, :], ALU.add), f"sa{q}")
                if q < 3:
                    o = take(f"st{q}").rearrange("p (c n) -> p c n", c=4)
                    for r in (0, 64):
                        rs = slice(r, r + 64)
                        d = ST[q + 1][rs, :, rs]
                        gate = GG[rs, :, q * CH + CH - 1:q * CH + CH].to_broadcast([64, 4, 64])
                        src = o[rs, :, rs]
                        if q:
                            step(tt(d, src, ST[q][rs, :, rs], ALU.add))
                            src = d
                        if r and q == 0:
                            release(tt(d, src, gate, ALU.mult), f"st{q}")
                        else:
                            step(tt(d, src, gate, ALU.mult))
                    if q:
                        V.memset(small[:, 122:123], 0.0).then_inc(free(f"st{q}"), 1)
                    else:
                        dve.wait_ge(*freed("st0"))
                    V.memset(small[:, 123:124], 0.0).then_inc(sem("state"), 1)
            for u in range(2):
                c = slice(2 * u, 2 * u + 2)
                release(stt(YT[:, c, :], take(f"mean{u}").rearrange("p (c n) -> p c n", c=2), -1.0 / 64,
                            YT[:, c, :], ALU.mult, ALU.add), f"mean{u}")
            dve.wait_ge(*freed("var1"))
            dve.wait_ge(*freed("var0"))
            step(V.reciprocal(YQ, YQ))
            step(tt(YT, YT, YQ, ALU.mult))
            for c in range(4):
                mark(V.tensor_scalar(YT[:, c, :], YT[:, c, :], pcol("lg", c), pcol("lb", c), ALU.mult, ALU.add))
            settle()
            dve.wait_ge(*freed("bon1"))
            step(tt(YT, YT, BN, ALU.add))
            tt(ys[:, 0:4, :], YT, GT, ALU.mult).then_inc(sem("ys"), 1)
            for m in range(KD):
                for n in range(3):
                    name = f"br{m}.{n}"
                    o = take(name)
                    ready(dve, "gate", 3 * m + n + 1)
                    g = sgm[:, (3 * m + n) % 2, :]
                    if n == 0:
                        release(tt(mg[:, m, :], g, o[:, T:2 * T], ALU.mult), name)
                        dve.wait_ge(*freed(name))
                        continue
                    release(tt(prod, g, o[:, T:2 * T], ALU.mult), name)
                    dve.wait_ge(*freed(name))
                    if n == 1:
                        step(tt(mg[:, m, :], mg[:, m, :], prod, ALU.add))
                    else:
                        tt(mg[:, m, :], mg[:, m, :], prod, ALU.add).then_inc(sem("merged"), 1)
                        ready(dve, "merged", m + 1)

            def residual(names, s):
                for u, name in enumerate(names):
                    c = slice(2 * u, 2 * u + 2)
                    step(tt(xT[:, c, :], xT[:, c, :], take(name).rearrange("p (c n) -> p c n", c=2), ALU.add))
                    V.memset(small[:, 124:125], 0.0).then_inc(free(name), 1)
                    V.memset(small[:, 125:126], 0.0).then_inc(sem(s), 1)

            def ffn(f, rms_, g, s):
                norm(f"f{f}", rms_, xT, hT, g, rstd)
                a0 = unit[f"up{f}.0"][1]

                def up(i, j):
                    ai = a0 + j
                    u = i * 4 + j
                    dve.wait_ge(sem(f"fullA{ai % 4}"), i + ai // 4 + 1)
                    ready(dve, "tap2", u * 2 + (f * UPS * 2 + 2))
                    for back in (1, 2):
                        for m in range(2):
                            cc = u * 2 + (PCOL[f"cw{f}"] + (2 - back) * 2 * KF + m)
                            d = acc[:, j % 2, m * T + back:(m + 1) * T]
                            last = stt(d, psA[ai % 4][:, m * T:(m + 1) * T - back], par[:, bass.ds(cc, 1)], d,
                                       ALU.mult, ALU.add)
                            last.then_inc(sem(f"taps"), 1)
                        dve.wait_ge(sem("taps"), u * 4 + (f * UPS * 4 + 2 * back))
                    V.memset(small[:, 126:127], 0.0).then_inc(sem(f"freeA{ai % 4}"), 1)
                    V.memset(small[:, 127:128], 0.0).then_inc(sem("conv"), 1)
                up_loop(dve, up)
                residual([f"down{f}.{u}" for u in range(4)], s)
            residual([f"wo{u}" for u in range(4)], "x1")
            ffn(0, "r2", "n2", "x2")

            norm("l", "r3", xT, hT, "an", rstd)
            o = take("gt")
            mark(V.tensor_scalar(rowG[0:4, :], o[0:4, 0:T], pcol("bi", 0, 4), None, ALU.add))
            settle()
            release(V.tensor_scalar(rowLF[0:4, :], o[0:4, T:2 * T], pcol("bf", 0, 4), None, ALU.add), "gt")
            dve.wait_ge(*freed("gt"))
            V.memset(small[:, 119:120], 0.0).then_inc(sem("f_row"), 1)
            ready(dve, "f_ln")
            step(stt(rowLF[0:4, :], rowLF[0:4, :], 0.0, rowT[0:4, :], ALU.min, ALU.subtract))
            step(V.tensor_tensor_scan(rowF[0:4, :], cst("one", 4), rowLF[0:4, :], 0.0, ALU.mult, ALU.add))
            tt(rowG[0:4, :], rowG[0:4, :], rowF[0:4, :], ALU.subtract).then_inc(sem("g_row"), 1)
            ready(dve, "g_row")
            step(V.tensor_tensor_scan(rowM2[0:4, 0:T], cst("one", 4), rowG[0:4, :], 0.0, ALU.mult, ALU.max))
            tt(rowM2[0:4, T:2 * T], rowM2[0:4, 0:T], rowF[0:4, :], ALU.add).then_inc(sem("m_row"), 1)
            for h in range(4):
                o = take(f"mb{h}")
                if h >= 2:
                    dve.wait_ge(*freed(f"sc{h - 2}"))
                mark(tt(ET[:, h % 2, 0:T], o[:, 0:T], cst("posI"), ALU.add))
                settle()
                tt(ET[:, h % 2, T:T + P], o[:, P:T], cst("posI")[:, 0:P], ALU.add).then_inc(sem("e_in"), 1)
                ready(dve, "e_out", h + 1)
                release(tt(SS[:, h % 2, :], ET[:, h % 2, :], take(f"sc{h}")[:, 0:384], ALU.mult), f"sc{h}")
                dve.wait_ge(*freed(f"dn{h}"))
                dve.wait_ge(*freed(f"mb{h}"))
                d = dn[:, h % 2, :]
                step(tt(d, d, EM[:, h % 2, :], ALU.max))
                V.reciprocal(d, d).then_inc(sem("l_den"), 1)
                ready(dve, "l_den", h + 1)
                o = take(f"nm{h}")
                for e in range(2):
                    tt(hr[:, 2 * h + e, :], o[:, e * T:(e + 1) * T], d, ALU.mult).then_inc(sem("l_hr"), 1)
                ready(dve, "l_hr", 2 * h + 2)
                V.memset(small[:, 118:119], 0.0).then_inc(free(f"nm{h}"), 1)
            for u in range(2):
                dve.wait_ge(*freed(f"hn{u}"))
                step(V.reciprocal(hsd[:, 2 * u:2 * u + 2, :], hsd[:, 2 * u:2 * u + 2, :]))
            for h in range(4):
                for e in range(2):
                    c = 2 * h + e
                    mark(stt(hr[:, c, :], hr[:, c, :], pcol("ah", c), hsd[:, h, :], ALU.mult, ALU.mult))
            settle()
            for c in range(KD):
                if c % 2 == 0:
                    dve.wait_ge(*freed(f"lo{c // 2}"))
                tt(hr[:, c, :], hr[:, c, :], og[:, c, :], ALU.mult).then_inc(sem("l_h"), 1)
            residual([f"aw{u}" for u in range(4)], "x3")
            ffn(1, "r4", "f0", "x4")

            norm("a", "r5", xT, hT, "kvn", rstd)
            for k in range(KD):
                stt(h2[:, k, :], xT[:, k, :], pcol("bn", k), rstd, ALU.mult, ALU.mult).then_inc(sem("h_b"), 1)
            for x, dst, g in (("k", ak, "kn"), ("q", aq, "bq")):
                head_norm(asq, dst, [f"b{x}n{u}" for u in range(4)], [pcol(g)] * 4, "a_n")
                n0 = 0 if x == "k" else 4
                for u in range(4):
                    c = slice(2 * u, 2 * u + 2)
                    name = f"b{x}r{u}"
                    release(tt(asq[:, c, :], take(name).rearrange("p (c n) -> p c n", c=2),
                               bc(cst("sin"), 2), ALU.mult), name)
                    dve.wait_ge(*freed(name))
                    ready(dve, "a_cos", n0 + u + 1)
                    tt(dst[:, c, :], asq[:, c, :], atm[:, c, :], ALU.add).then_inc(sem("a_rope"), 1)

            def a_max(h):
                if h >= 2:
                    ready(dve, "a_e", 2 * (h - 1))
                o = take(f"as{h}")
                s_ = aS[:, h % 2, :]
                release(tt(s_, o[:, 0:384], cst("negC"), ALU.add), f"as{h}")
                dve.wait_ge(*freed(f"as{h}"))
                mark(V.tensor_reduce(small[:, 40 + 2 * h:41 + 2 * h], s_[:, 0:P], AX.X, ALU.max))
                mark(V.tensor_reduce(small[:, 41 + 2 * h:42 + 2 * h], s_[:, P:3 * P], AX.X, ALU.max))
                settle()
                V.tensor_scalar(small[:, 56 + 2 * h:58 + 2 * h], small[:, 40 + 2 * h:42 + 2 * h], -P ** -0.5,
                                None, ALU.mult).then_inc(sem("a_max"), 1)
            a_max(0)
            for h in range(8):
                if h < 7:
                    a_max(h + 1)
                ready(dve, "a_e", 2 * h + 2)
                rs = small[:, 72 + 2 * h:74 + 2 * h]
                step(V.reciprocal(rs, rs))
                p_ = aP[:, h % 2, :]
                step(V.tensor_scalar(p_[:, 0:P], p_[:, 0:P], rs[:, 0:1], None, ALU.mult))
                V.tensor_scalar(p_[:, P:3 * P], p_[:, P:3 * P], rs[:, 1:2], None, ALU.mult)\
                    .then_inc(sem("a_p"), 1)
            residual([f"bo{u}" for u in range(4)], "x5")
            ffn(2, "r6", "f1", "x_final")


def feature_blocks(w):
    k, n = w.shape
    return w.reshape(k // P, P, n // P, P).transpose(2, 0, 1, 3).reshape(-1, P, P)


def token_blocks(w):
    k, n = w.shape
    return w.reshape(k // P, P, n // 512, 4, P).transpose(2, 0, 3, 1, 4).reshape(-1, P, P)


def pairs(w, swap):
    k = w.shape[0]
    v = w.reshape(k, 2, KF, P)
    if swap:
        v = v[:, ::-1]
    return v.transpose(0, 2, 1, 3).reshape(k, 2 * KF * P)


def kernel(**inputs):
    import concourse.bacc as bacc
    from concourse.bass_utils import run_bass_kernel_spmd

    a = {k: np.asarray(v) for k, v in inputs.items() if np.asarray(v).size}
    w_in, kv = a["w_in"][0], a["w_mem_kv"][0]
    cut = np.cumsum([0, 1792, 512, 512, 512, 512, 3072])
    rw, sq, sk, sv, mq, gates = [w_in[:, cut[i]:cut[i + 1]] for i in range(6)]
    g_blocks = feature_blocks(gates).reshape(3, KD, KD, P, P)
    b_blocks = np.stack([feature_blocks(a["w_branch"][0, n]).reshape(KD, W4, P, P) for n in range(3)])
    merge = np.concatenate([g_blocks, b_blocks], 2).transpose(1, 0, 2, 3, 4).reshape(-1, P, P)
    aw = a["a_w_in_2"][0]

    def ffn(up, down, swap):
        return [feature_blocks(pairs(up, swap)), feature_blocks(down)]
    stream = ([feature_blocks(rw), feature_blocks(sq), feature_blocks(sk), token_blocks(sv),
               feature_blocks(mq), feature_blocks(kv[:, :512]), token_blocks(kv[:, 512:]), merge,
               feature_blocks(a["w_out"][0])] + ffn(a["w_up"][0], a["w_down"][0], False)
              + [feature_blocks(aw[:, 0:1024]), token_blocks(aw[:, 1024:2048]),
                 feature_blocks(aw[:, 2048:3072]), feature_blocks(a["a_w_out_2"][0])]
              + ffn(a["f_w_up_2"][0], a["f_w_down_2"][0], True)
              + [feature_blocks(a["w_kv_2"][:, :1024]), token_blocks(a["w_kv_2"][:, 1024:]),
                 feature_blocks(a["b_w_q_2"][0]), feature_blocks(a["b_w_o_2"][0])]
              + ffn(a["f_w_up_2"][1], a["f_w_down_2"][1], True))
    blocks = np.concatenate(stream)
    w = np.ascontiguousarray(blocks.reshape(-1, SLOT, P, P).transpose(0, 2, 1, 3)).reshape(-1, P, SLOT * P)

    par = np.zeros((P, NPAR), np.float32)

    def put(name, v):
        v = np.asarray(v).reshape(-1, P).T
        par[:, PCOL[name]:PCOL[name] + v.shape[1]] = v
    for name, v in (("n1", a["norm1_g"][0]), ("mg", a["mem_norm_g"][0]), ("mu", a["shift_mu"][0]),
                    ("w0", a["decay_w0"][0]), ("a0", a["iclr_a0"][0]), ("kk", a["k_k"][0]),
                    ("ka", a["k_a"][0]), ("rk", a["r_k"][0]), ("lg", a["lnx_g"][0]), ("lb", a["lnx_b"][0]),
                    ("sbq", np.tile(a["sb_q_norm_g"][0], 2)), ("sbk", np.tile(a["sb_k_norm_g"][0], 2)),
                    ("mq", a["mem_q_norm_g"][0]), ("mk", a["mem_k_norm_g"][0]), ("n2", a["norm2_g"][0]),
                    ("an", a["a_norm_2"][0]), ("ah", a["a_h_norm_2"][0]), ("kvn", a["kv_norm_2"]),
                    ("kn", a["k_norm_2"]), ("bn", a["b_norm_2"][0]), ("bq", a["b_q_norm_2"][0]),
                    ("f0", a["f_norm_2"][0]), ("f1", a["f_norm_2"][1])):
        put(name, v)
    par[0:4, PCOL["bi"]] = a["a_b_gates_2"][0, 0]
    par[0:4, PCOL["bf"]] = a["a_b_gates_2"][0, 1]
    for f, (cw, cb, swap) in enumerate(((a["conv_w"][0], a["conv_b"][0], False),
                                        (a["f_conv_w_2"][0], a["f_conv_b_2"][0], True),
                                        (a["f_conv_w_2"][1], a["f_conv_b_2"][1], True))):
        put(f"cw{f}", pairs(cw, swap))
        put(f"cb{f}", pairs(cb[None], swap))

    def major(v):
        return np.ascontiguousarray(v.T.reshape(-1, P, v.shape[0]).transpose(1, 0, 2))
    arrays = {
        "x": major(a["x"][0]), "mem": major(a["mem"][0]), "w": w, "par": par, "con": constants(),
        "decay_w2": a["decay_w2"][0], "iclr_a2": a["iclr_a2"][0], "gate_g2": a["gate_g2"][0],
        "wg": np.ascontiguousarray(aw[:, 3072:3080].reshape(KD, P, 8).transpose(1, 0, 2)),
    }
    arrays = {f"in_{k}": np.ascontiguousarray(v) for k, v in arrays.items()}
    nc = bacc.Bacc("TRN2", target_bir_lowering=False, num_devices=1)
    ins = {k[3:]: nc.dram_tensor(k, v.shape, F32, kind="ExternalInput").ap() for k, v in arrays.items()}
    out = nc.dram_tensor("out", (P, KD, T), F32, kind="ExternalOutput").ap()
    program(nc, ins, out)
    r = run_bass_kernel_spmd(nc, [arrays], core_ids=[0]).results[0]["out"]
    return r.reshape(P, KD, T).transpose(2, 1, 0).reshape(1, T, D)
```

```python
from contextlib import ExitStack

import concourse.bass as bass
from concourse import mybir
import numpy as np

F32 = mybir.dt.float32
F32R = mybir.dt.float32r
ALU = mybir.AluOpType
ACT = mybir.ActivationFunctionType
AX = mybir.AxisListType

P = 128
T = 256
TT = T // P
D = 1024
KD = D // P
FF = 2816
KF = FF // P
W4 = 512 // P
CH = 64
NEG = -1e30
SLOT = 8
RING = 8
HRING = 4
ORDER = (1, 2, 0)
DECAY = float(np.exp(-0.5))

PARAMS = [("n1", 8), ("mg", 8), ("mu", 14), ("w0", 4), ("a0", 4), ("kk", 4), ("ka", 4), ("rk", 4),
          ("lg", 4), ("lb", 4), ("sbq", 1), ("sbk", 1), ("mq", 1), ("mk", 1), ("n2", 8),
          ("an", 8), ("bi", 1), ("bf", 1), ("ah", 8), ("kvn", 8), ("kn", 1), ("bn", 8), ("bq", 1),
          ("f0", 8), ("f1", 8)]
for _f in range(3):
    PARAMS += [(f"cw{_f}", 3 * 2 * KF), (f"cb{_f}", 2 * KF)]
PCOL, _at = {}, 0
for _n, _k in PARAMS:
    PCOL[_n] = _at
    _at += _k
NPAR = _at

CONSTS = [("ident", P), ("ones", P), ("bones", P), ("mask4", 4 * P), ("lev", 6 * P), ("rev", P),
          ("negS", 3 * P), ("scan", T), ("eps", 2)]
CONSTS2 = [("posI", 2 * P), ("negC", 3 * P), ("cos", T), ("sin", T), ("rot", P), ("sel", 4 * P),
           ("one", T)]
CCOL, _at = {}, 0
for _n, _k in CONSTS + CONSTS2:
    CCOL[_n] = (_at, _k)
    _at += _k
NCON = _at
NCON1 = CCOL[CONSTS2[0][0]][0]


def constants():
    c = np.zeros((P, NCON), np.float32)

    def put(name, a):
        at, k = CCOL[name]
        c[:a.shape[0], at:at + k] = a
    i = np.arange(P)
    s, t = i[:, None], i[None, :]
    same = (s // CH) == (t // CH)
    put("ident", np.eye(P))
    put("ones", np.ones((P, P)))
    put("bones", same * 1.0)
    strict, incl = same & (s < t), same & (s <= t)
    put("mask4", np.concatenate([strict * 1.0, incl * 1.0, incl * 1.0, strict * -1.0], 1))
    lev = []
    for m in (1, 2, 4, 8, 16, 32):
        off = (s // (2 * m) == t // (2 * m)) & ((s // m) % 2 == 1) & ((t // m) % 2 == 0)
        lev.append(np.eye(P) - off)
    put("lev", np.concatenate(lev, 1))
    put("rev", (s >= t) * 1.0)
    z = np.zeros((P, P))
    put("negS", np.concatenate([(s >= t) * NEG, z, (s >= t) * NEG], 1))
    put("posI", np.concatenate([(s > t) * -NEG, z], 1))
    put("negC", np.concatenate([(t > s) * NEG, z, (t > s) * NEG], 1))
    half = 16
    inv = 500000.0 ** (-np.arange(0, 32, 2, dtype=np.float32) / np.float32(32))
    ang = np.arange(T, dtype=np.float32)[None, :] * inv.astype(np.float32)[:, None]
    cos, sin = np.ones((P, T)), np.zeros((P, T))
    cos[:half] = cos[half:2 * half] = np.cos(ang)
    sin[:half] = sin[half:2 * half] = np.sin(ang)
    put("cos", cos)
    put("sin", sin)
    rot = np.zeros((P, P))
    for m in range(half):
        rot[m + half, m] = -1.0
        rot[m, m + half] = 1.0
    put("rot", rot)
    put("scan", np.tile((np.arange(T) % CH != 0) * 1.0, (P, 1)))
    sel = np.zeros((4, 4 * P))
    for h in range(4):
        sel[h, h * P:(h + 1) * P] = 1.0
    put("sel", sel)
    put("one", np.ones((P, T)))
    put("eps", np.tile(np.array([[1e-6, 64e-5]]), (P, 1)))
    return c


def ffn_units(f):
    return [f"up{f}.{u}" for u in range(KF)] + [f"down{f}.{u}" for u in range(KD // 2)]


LIN = ([f"rw{u}" for u in range(7)] + ["sq0", "sq1", "sk0", "sk1", "sv0", "sv1", "mq0", "mq1",
       "mk0", "mk1", "mv0", "mv1"] + [f"br{m}.{n}" for m in range(KD) for n in ORDER]
       + [f"wo{u}" for u in range(4)] + ffn_units(0)
       + ["lq0", "lq1", "lk0", "lk1", "lv00", "lv01", "lv10", "lv11", "lo0", "lo1", "lo2", "lo3"]
       + [f"aw{u}" for u in range(4)] + ffn_units(1)
       + [f"bq{u}" for u in range(4)] + [f"bk{u}" for u in range(4)] + ["bv00", "bv01", "bv10", "bv11"]
       + [f"bo{u}" for u in range(4)] + ffn_units(2))
def slot_ends():
    ends, blocks = {}, 0
    for i, n in enumerate(LIN):
        token = n in ("sv0", "sv1", "mv0", "mv1") or n[:2] in ("lv", "bv")
        blocks += 12 if n.startswith("br") else 2 * KF if n.startswith("down") else 2 * KD
        ends[n] = -(-blocks // SLOT)
        if token and n[-1] == "1":
            ends[LIN[i - 1]] = ends[n]
    return ends


SLOT_END = slot_ends()

SM = (["rx", "rm", "dl0", "dl1", "al0", "al1", "gl0", "gl1", "kn0", "kn1",
       "sqn0", "sqn1", "skn0", "skn1", "mqn0", "mqn1", "mkn0", "mkn1", "bon0", "bon1"]
      + [f"z{h}" for h in range(8)] + [f"cs{h}" for h in range(8)] + [f"so{c}" for c in range(4)])
SM += ["ms0"]
for _h in range(4):
    SM += ([f"ms{_h + 1}"] if _h < 3 else []) + [f"mt{_h}", f"mo{_h}"]
SM += [f"tr{t}.{n}" for t in range(TT) for n in "vbka"]
SM += [f"qd{i}" for i in range(16)] + [f"mm{t}" for t in range(TT)]
SM += [f"l0x{g}" for g in range(4)] + [f"l0t{g}" for g in range(4)]
for _l in range(1, 6):
    SM += [f"l{_l}p{g}" for g in range(4)]
    SM += [n for g in range(4) for n in (([f"l{_l}x{g}"] if _l < 5 else []) + [f"l{_l}t{g}"])]
SM += [n for t in range(TT) for n in (f"ut{t}.0", f"ut{t}.1", f"zz{t}")]
for _q in range(4):
    SM += ([f"sa{_q}"] if _q else []) + ([f"st{_q}"] if _q < 3 else [])
SM += [f"y{c}" for c in range(4)] + ["mean0", "mean1", "var0", "var1"]
SM += ["r2", "r3", "gt", "gcol"]
for _h in range(4):
    SM += [f"mb{_h}", f"sc{_h}", f"dn{_h}", f"nm{_h}"]
SM += ["hn0", "hn1", "r4", "r5"]
SM += [f"b{_n}{u}" for _n in ("qn", "qr", "kn", "kr") for u in range(4)]
SM += ["as0", "as1"]
for _h in range(8):
    SM += ([f"as{_h + 2}"] if _h < 6 else []) + [f"at{_h}", f"ao{_h}"]
SM += ["r6"]


def program(nc, ins, out):
    ctx = ExitStack()
    with ctx:
        sems = {}

        def sem(name):
            if name not in sems:
                sems[name] = ctx.enter_context(nc.semaphore(name))
            return sems[name]

        psA = [ctx.enter_context(nc.psum_tensor(f"psA{i}", [P, 512], F32)) for i in range(4)]
        psB = [ctx.enter_context(nc.psum_tensor(f"psB{i}", [P, 512], F32)) for i in range(4)]
        unit = {n: ("A", i) for i, n in enumerate(LIN)}
        unit.update({n: ("B", i) for i, n in enumerate(SM)})
        assert len(unit) == len(LIN) + len(SM)

        def bank(name):
            r, i = unit[name]
            return (psA if r == "A" else psB)[i % 4]

        def full(name):
            r, i = unit[name]
            return sem(f"full{r}{i % 4}"), i // 4 + 1

        def free(name):
            r, i = unit[name]
            return sem(f"free{r}{i % 4}")

        def freed(name):
            return free(name), unit[name][1] // 4 + 1

        KB = 256
        ARENA = 201
        MID = 104.5
        arena = ctx.enter_context(nc.sbuf_tensor("arena", [P, int(MID * KB)], F32))
        arena2 = ctx.enter_context(nc.sbuf_tensor("arena2", [P, int((ARENA - MID) * KB)], F32))
        start = nc.sbuf_base - ARENA * KB * 4
        places = [(4 * i, 4 * i + 4) for i in range(RING + HRING)] + [
            (62.5, 70.5), (70.5, 78.5), (78.5, 90.5), (90.5, 102.5), (104.5, 126.5), (126.5, 148.5),
            (152.5, 160.5), (160.5, 168.5), (168.5, 176.5), (176.5, 184.5)]
        rounded = [nc.alloc_sbuf_tensor_at(f"rounded{i}", [P, int((b - a) * KB)], F32R,
                                           offset=start + int(a * 1024)) for i, (a, b) in enumerate(places)]

        def view(kb, c, n, off=0):
            at = int(kb * KB) + off
            half = int(MID * KB)
            assert at >= half or at + c * n <= half
            v = arena[:, at:at + c * n] if at < half else arena2[:, at - half:at - half + c * n]
            return v.rearrange("p (c n) -> p c n", c=c) if c > 1 else v

        ring = [view(4 * i, 1, SLOT * P) for i in range(RING)]
        upper = [view(32 + 4 * i, 1, SLOT * P) for i in range(HRING)]
        con1 = view(48, 1, NCON1)
        par = view(57.75, 1, NPAR)
        assert NCON1 <= 9.75 * KB and NPAR <= 2.75 * KB
        small = view(60.5, 1, 128)
        rstd = view(61, 1, T)
        wgate = view(62, KD, 8)
        HH = view(62.5, KD, T)
        HL = view(70.5, KD, T)
        base = 78.5
        ys = view(base, 12, T)
        pb = view(base + 12, 14, T)
        YH = view(base + 12, 12, T)
        T2 = view(base + 12, 4, 512)
        r0 = base + 26
        SG = view(r0, 4, T)
        LC = view(r0 + 4, 4, T)
        AA = view(r0 + 8, 4, T)
        GG = view(r0 + 12, 4, T)
        lora = view(r0 + 12, 1, 1024)
        K1 = view(r0 + 16, 4, T)
        AR = view(r0 + 20, 8, T)
        KM = view(r0 + 28, 4, T)
        BN = view(r0 + 32, 4, T)
        GT = view(r0 + 36, 4, T)
        sq1 = view(r0 + 28, KD, T)
        rstdm = view(r0 + 36, 1, T)
        ST = [None, view(r0, 4, P), view(r0, 4, P, 512), view(r0 + 28, 4, P)]
        UT = view(r0 + 20, 4, T)
        ZZ = view(r0 + 16, TT, 512)
        MM = view(r0 + 4, TT, 512)
        SA = view(r0 + 8, TT, 512)
        z0 = r0 + 40
        z1 = z0 + 16
        mv = view(z0, TT, 512)
        sbv = view(z0 + 4, TT, 512)
        memH = view(z0 + 8, KD, T)
        tok = view(z0, 8, 512)
        sgm = view(z0, 2, T)
        prod = view(z0 + 2, 1, T)
        sbqk = view(z1, 8, T)
        mqk = view(z1 + 8, 8, T)
        zb = view(z1 + 16, 8, 384)
        memT = view(z1 + 16, KD, T)
        mP = view(z1 + 16, 2, 512)
        mPT = view(z1 + 20, 2, 512)
        eb = view(z1 + 28, 8, 384)
        sqs = view(z1 + 16, 8, T)
        sqm = view(z1 + 28, 8, T)
        quad = view(z1, 16, 384)
        MP = view(z1 + 24, 16, P)
        X = view(z1 + 24, 4, 512)
        XT = view(z1 + 32, 4, 512)
        YT = view(z1 + 24, 4, T)
        YQ = view(z1 + 28, 4, T)
        xT = view(z1 + 32, KD, T)
        mg = view(z1, KD, T)
        mgH = view(z1 + 8, KD, T)
        AH = view(r0, KF, T)
        AL = view(r0 + 22, KF, T)
        acc = view(z0 + 4, 2, 512)
        sil = view(z0 + 8, 2, T)
        gv = view(z0 + 10, 2, T)
        sq8 = view(z1, KD, T)
        assert z1 + 40 <= ARENA
        lqk = view(base, 8, T)
        lv = view(base + 8, TT, D)
        og = view(base + 16, KD, T)
        rowLF = view(base + 24, 1, T)
        rowF = view(base + 25, 1, T)
        rowG = view(base + 26, 1, T)
        rowM2 = view(base + 27, 1, 2 * T)
        rowT = view(base + 29, 1, T)
        EM = view(base + 30, 2, T)
        ET = view(base + 32, 2, 384)
        SS = view(base + 35, 2, 384)
        dn = view(base + 38, 2, T)
        hr = view(base + 40, KD, T)
        sq2 = view(base + 48, KD, T)
        hsd = view(base + 56, 4, T)
        hrH = view(base + 60, KD, T)
        h2H = view(base, KD, T)
        h2L = view(z1 + 8, KD, T)
        ak = view(base + 8, KD, T)
        aq = view(base + 16, KD, T)
        av = view(base + 26, TT, D)
        ao = view(base + 34, KD, T)
        aoH = view(base + 74, KD, T)
        con2 = view(z1 + 24, 1, NCON - NCON1)
        asq = {"q": view(base + 42, KD, T), "k": view(z1, KD, T)}
        atm = {"q": view(base + 50, KD, T), "k": view(z1 + 16, KD, T)}
        aS = view(base + 58, 3, 384)
        aP = view(base + 62.5, 3, 384)
        aPT = view(base + 67, 2, 384)

        def cst(name, rows=P):
            at, k = CCOL[name]
            if at >= NCON1:
                return con2[0:rows, at - NCON1:at - NCON1 + k]
            return con1[0:rows, at:at + k]

        def pcol(name, i=0, rows=P):
            return par[0:rows, PCOL[name] + i:PCOL[name] + i + 1]

        ident, ones, bones = cst("ident"), cst("ones"), cst("bones")
        eps6, epsln = con1[:, CCOL["eps"][0]:CCOL["eps"][0] + 1], con1[:, CCOL["eps"][0] + 1:CCOL["eps"][0] + 2]
        omm = small[:, 0:14]
        PRE = SLOT_END["mv1"] + 3
        UPS = KF

        def fr(ap):
            first = ap.tensor.name == arena.name
            row = int(MID * KB) if first else int((ARENA - MID) * KB)
            part_, at = ap.offset // row, ap.offset % row + (0 if first else int(MID * KB))
            for (a, b), place in zip(places, rounded):
                if a * KB <= at < b * KB:
                    w = int((b - a) * KB)
                    return bass.AP(tensor=place, offset=part_ * w + at - int(a * KB),
                                   ap=[[w, ap.ap[0][1]]] + [list(x) for x in ap.ap[1:]])
            raise AssertionError(at / KB)

        def rd(ap):
            return fr(ap).bitcast(F32)

        def bc(ap, n):
            return ap.unsqueeze(1).to_broadcast([ap.shape[0], n, ap.shape[1]])

        def ready(eng, name, n=1):
            eng.wait_ge(sem(name), n)

        def up_loop(eng, body):
            for j in range(4):
                body(0, j)
            with eng.Fori(1, UPS // 4) as i:
                for j in range(4):
                    body(i, j)
            for j in range(UPS % 4):
                body(UPS // 4, j)

        block = ctx.enter_context(nc.Block())

        @block.sync
        def _(sp):
            sp.dma_start(xT, ins["x"]).then_inc(sem("ld_x"), 16)
            sp.dma_start(con1, ins["con"][:, 0:NCON1]).then_inc(sem("ld_con"), 16)
            nslots = ins["w"].shape[0]
            assert nslots % RING == 0

            def slot(i, j):
                sp.dma_start(ring[j], ins["w"][bass.ds(i * RING + j, 1), :, :]
                             .rearrange("a p n -> p (a n)")).then_inc(sem(f"w{j}"), 16)
            for j in range(RING):
                slot(0, j)
            with sp.Fori(1, nslots // RING) as i:
                for j in range(RING):
                    sp.wait_ge(sem("slots_used"), i * RING + (j - RING + 1))
                    slot(i, j)
            ready(sp, "x_final", 4)
            sp.dma_start(out, xT).then_inc(sem("stored"), 16)
            sp.wait_ge(sem("stored"), 16)

        @block.tensor
        def _(pe):
            state = {"slot": 0, "blk": 0, "A": 0, "B": 0, "inc": False}

            def mm(o, l, r, start, stop):
                ins_ = nc.tensor.matmul(o, l, r, start=start, stop=stop)
                if state["inc"]:
                    ins_.then_inc(sem("slots_used"), 1)
                    state["inc"] = False
                return ins_

            def weights(n):
                s, b = state["slot"], state["blk"]
                if b == 0:
                    pe.wait_ge(sem("w_rest"), s + 1)
                    state["inc"] = s > 0
                state["blk"] = b + n
                if state["blk"] == SLOT:
                    state["slot"], state["blk"] = s + 1, 0
                c = slice(b * P, (b + n) * P)
                return fr(upper[s % HRING][:, c]), fr(ring[s % RING][:, c])

            def mm3(o, w, x, start, stop, turn=False):
                for n, (a, b) in enumerate(((0, 0), (1, 0), (0, 1))):
                    l, m = (x[b], w[a]) if turn else (w[a], x[b])
                    last = mm(o, l, m, start and n == 0, stop and n == 2)
                return last

            def part(x, *at):
                return fr(x[0][at]), fr(x[1][at])

            def open_(name):
                r, i = unit[name]
                assert state[r] == i, (name, i, state[r])
                state[r] += 1
                if i >= 4:
                    pe.wait_ge(free(name), i // 4)
                return bank(name)

            def close(ins_, name):
                ins_.then_inc(full(name)[0], 1)

            def project(names, src, wait=None, nk=KD):
                for n, name in enumerate(names):
                    o = open_(name)
                    for m in range(2):
                        for k in range(nk):
                            w = weights(1)
                            if wait and n == 0 and m == 0:
                                pe.wait_ge(sem(wait), k + 1)
                            last = mm3(o[:, m * T:(m + 1) * T], w, part(src, slice(0, P), k), k == 0, k == nk - 1)
                    close(last, name)

            def project_tok(names, src, wait=None):
                o = [open_(n) for n in names]
                for k in range(KD):
                    w = weights(4)
                    if wait:
                        pe.wait_ge(sem(wait), k + 1)
                    for t in range(TT):
                        last = mm3(o[t][:, :], w, part(src, slice(0, P), k, slice(t * P, (t + 1) * P)),
                                   k == 0, k == KD - 1, turn=True)
                        if k == KD - 1:
                            close(last, names[t])

            def sum_squares(name, tag, sq):
                o = open_(name)
                ready(pe, f"sq_{tag}")
                for k in range(KD):
                    last = mm(o[:, 0:T], ones, sq[:, k, :], k == 0, k == KD - 1)
                close(last, name)

            def reduce_pairs(names, lhs, src, s, n0=0):
                for u, name in enumerate(names):
                    o = open_(name)
                    ready(pe, s, n0 + u + 1)
                    close(mm(o[:, :], lhs, src[:, 2 * u:2 * u + 2, :], True, True), name)

            pe.wait_ge(sem("ld_con"), 16)
            H, M = (HH, HL), (memH, memT)
            sum_squares("rx", "x", sq1)
            sum_squares("rm", "m", sq1)
            project([f"rw{u}" for u in range(7)], H, "h_x")
            project(["sq0", "sq1"], H)
            pe.wait_ge(sem("ld_lora"), 48)
            for name, lo, hi, col, ch, need in (("dl", 0, 64, 0, 12, 1), ("al", 64, 128, 0, 12, 1),
                                               ("gl", 0, 128, 512, 13, 2)):
                for u in range(2):
                    o = open_(f"{name}{u}")
                    ready(pe, "lora_in", need)
                    for m in range(2):
                        c = 2 * u + m
                        last = mm(o[:, m * T:(m + 1) * T], lora[lo:hi, col + c * P:col + (c + 1) * P],
                                  pb[lo:hi, ch, :], True, True)
                    close(last, f"{name}{u}")
            reduce_pairs(["kn0", "kn1"], bones, BN, "kk_sq")
            project(["sk0", "sk1"], H)
            project_tok(["sv0", "sv1"], H)
            project(["mq0", "mq1"], H)
            project(["mk0", "mk1"], M, "h_m")
            project_tok(["mv0", "mv1"], M)
            reduce_pairs(["sqn0", "sqn1", "skn0", "skn1"], bones, sqs, "sb_sq")
            reduce_pairs(["mqn0", "mqn1", "mkn0", "mkn1"], ones, sqm, "mem_sq")
            reduce_pairs(["bon0", "bon1"], bones, BN, "bonus_in")
            for h in range(8):
                c, b = h // 2, 64 * (h % 2)
                o = open_(f"z{h}")
                if h == 0:
                    ready(pe, "sb_n", 4)
                mm(o[:, 0:T], sbqk[b:b + 64, 4 + c, 0:P], sbqk[b:b + 64, c, :], True, True)
                close(mm(o[:, T:T + P], sbqk[b:b + 64, 4 + c, P:T], sbqk[b:b + 64, c, P:T], True, True),
                      f"z{h}")
            for h in range(8):
                o = open_(f"cs{h}")
                ready(pe, "sb_sp", h // 4 + 1)
                mm(o[:, 0:384], cst("rev"), eb[:, h, :], True, False)
                close(mm(o[:, P:T], ones, eb[:, h, T:T + P], False, True), f"cs{h}")
            for c in range(4):
                o = open_(f"so{c}")
                ready(pe, "sb_p", c // 2 + 1)
                for hh in range(2):
                    mm(o[:, hh * T:(hh + 1) * T], sbv[:, 0, c * P:(c + 1) * P], zb[:, 2 * c + hh, 0:T],
                       True, False)
                    last = mm(o[:, hh * T + P:(hh + 1) * T], sbv[:, 1, c * P:(c + 1) * P],
                              zb[:, 2 * c + hh, T:T + P], False, True)
                close(last, f"so{c}")

            def mem_scores(h):
                o = open_(f"ms{h}")
                if h == 0:
                    ready(pe, "mem_n", 4)
                for t in range(TT):
                    last = mm(o[:, t * T:(t + 1) * T], mqk[:, h, t * P:(t + 1) * P], mqk[:, 4 + h, :],
                              True, True)
                close(last, f"ms{h}")
            mem_scores(0)
            for h in range(4):
                if h < 3:
                    mem_scores(h + 1)
                o = open_(f"mt{h}")
                ready(pe, "mem_p", h + 1)
                for m in range(2):
                    for t in range(TT):
                        last = nc.tensor.transpose(o[:, (2 * m + t) * P:(2 * m + t + 1) * P],
                                                   mP[:, h % 2, t * T + m * P:t * T + (m + 1) * P], ident)
                close(last, f"mt{h}")
                o = open_(f"mo{h}")
                pe.wait_ge(*freed(f"mt{h}"))
                for m in range(2):
                    last = mm(o[:, 0:T], mv[:, m, h * P:(h + 1) * P], mPT[:, h % 2, m * T:(m + 1) * T],
                              m == 0, m == 1)
                close(last, f"mo{h}")

            for t in range(TT):
                for n, src in (("v", pb[:, 8:12, :]), ("b", K1), ("k", LC), ("a", AR[:, 0:4, :])):
                    name = f"tr{t}.{n}"
                    o = open_(name)
                    if t == 0:
                        ready(pe, "fm", {"v": 1, "a": 1, "b": 2, "k": 3}[n])
                    for c in range(4):
                        last = nc.tensor.transpose(o[:, c * P:(c + 1) * P], src[:, c, t * P:(t + 1) * P],
                                                   ident)
                    close(last, name)
            ARv = AR.rearrange("p (a c) n -> p a c n", a=2)
            for i in range(16):
                t, h = i // 8, i % 8
                c, b = h // 2, 64 * (h % 2)
                o = open_(f"qd{i}")
                ts = slice(t * P, (t + 1) * P)
                mm(o[:, 0:T], K1[b:b + 64, c, ts], ARv[b:b + 64, :, c, ts], True, True)
                for m in (0, 1):
                    last = mm(o[:, (2 + m) * P:(3 + m) * P], LC[b:b + 64, c, ts],
                              ARv[b:b + 64, 1 - m, c, ts], True, True)
                close(last, f"qd{i}")
            for t in range(TT):
                o = open_(f"mm{t}")
                pe.wait_ge(*freed(f"tr{t}.v"))
                for h in range(8):
                    if h % 4 == 0:
                        pe.wait_ge(*freed(f"qd{t * 8 + h + 3}"))
                    last = mm(o[:, h * 64:(h + 1) * 64], MP[:, t * 8 + h, :],
                              tok[:, t * 4, h * 64:(h + 1) * 64], True, True)
                close(last, f"mm{t}")
            for g in range(4):
                o = open_(f"l0x{g}")
                ready(pe, "LT", g + 1)
                for i in range(4):
                    last = mm(o[:, i * P:(i + 1) * P], quad[:, 4 * g + i, 0:P], ident, True, True)
                close(last, f"l0x{g}")
            for g in range(4):
                o = open_(f"l0t{g}")
                pe.wait_ge(*freed(f"l0x{g}"))
                for i in range(4):
                    last = nc.tensor.transpose(o[:, i * P:(i + 1) * P], X[:, g, i * P:(i + 1) * P], ident)
                close(last, f"l0t{g}")
            for l in range(1, 6):
                for g in range(4):
                    o = open_(f"l{l}p{g}")
                    pe.wait_ge(*freed(f"l{l - 1}x{g}"))
                    for i in range(4):
                        last = mm(o[:, i * P:(i + 1) * P], quad[:, 4 * g + i, 0:P],
                                  X[:, g, i * P:(i + 1) * P], True, True)
                    close(last, f"l{l}p{g}")
                for g in range(4):
                    pe.wait_ge(*freed(f"l{l}p{g}"))
                    pe.wait_ge(*freed(f"l{l - 1}t{g}"))
                    if l < 5:
                        o = open_(f"l{l}x{g}")
                        for i in range(4):
                            s = slice(i * P, (i + 1) * P)
                            last = mm(o[:, s], XT[:, g, s], T2[:, g, s], True, True)
                        close(last, f"l{l}x{g}")
                    o = open_(f"l{l}t{g}")
                    for i in range(4):
                        s = slice(i * P, (i + 1) * P)
                        last = mm(o[:, s], T2[:, g, s], XT[:, g, s], True, True)
                    close(last, f"l{l}t{g}")

            def XTt(i):
                return XT[:, i // 4, (i % 4) * P:(i % 4 + 1) * P]
            for t in range(TT):
                for cp in range(2):
                    o = open_(f"ut{t}.{cp}")
                    pe.wait_ge(*freed(f"l5t{2 * t + cp}"))
                    pe.wait_ge(*freed(f"tr{t}.a"))
                    for j in range(4):
                        last = mm(o[:, j * P:(j + 1) * P],
                                  tok[:, t * 4 + 3, (2 * cp + j // 2) * P:(2 * cp + j // 2 + 1) * P],
                                  XTt(t * 8 + 4 * cp + j), True, True)
                    close(last, f"ut{t}.{cp}")
                o = open_(f"zz{t}")
                pe.wait_ge(*freed(f"mm{t}"))
                for h in range(8):
                    last = mm(o[:, h * 64:(h + 1) * 64], XTt(t * 8 + h), MM[:, t, h * 64:(h + 1) * 64],
                              True, True)
                close(last, f"zz{t}")
            for q in range(4):
                t, hs = q // 2, slice(CH * (q % 2), CH * (q % 2) + CH)
                if q:
                    o = open_(f"sa{q}")
                    pe.wait_ge(*freed(f"ut{t}.0"))
                    pe.wait_ge(*freed(f"ut{t}.1"))
                    ready(pe, "state", q)
                    for c in range(4):
                        last = mm(o[:, c * P:(c + 1) * P], UT[:, c, t * P:(t + 1) * P], ST[q][:, c, :],
                                  True, True)
                    close(last, f"sa{q}")
                if q < 3:
                    o = open_(f"st{q}")
                    if q:
                        pe.wait_ge(*freed(f"sa{q}"))
                    else:
                        ready(pe, "SA0")
                    for c in range(4):
                        s = slice(c * P, (c + 1) * P)
                        mm(o[:, s], tok[hs, t * 4 + 1, s], SA[hs, t, s], True, False)
                        last = mm(o[:, s], tok[hs, t * 4 + 2, s], tok[hs, t * 4, s], False, True)
                    close(last, f"st{q}")
            pe.wait_ge(*freed("sa3"))
            for c in range(4):
                o = open_(f"y{c}")
                cs = slice(c * P, (c + 1) * P)
                for hh in range(2):
                    for t in range(TT):
                        i = t * 8 + 2 * c + hh
                        s = slice(hh * T + t * P, hh * T + (t + 1) * P)
                        mm(o[:, s], SA[:, t, cs], quad[:, i, P:T], True, False)
                        mm(o[:, s], tok[:, t * 4, cs], quad[:, i, 2 * P:3 * P], False, False)
                        for q in range(max(2 * t, 1), 2 * t + 2):
                            last = mm(o[:, hh * T + q * CH:hh * T + (q + 1) * CH], ST[q][:, c, :],
                                      AR[:, 4 + c, q * CH:(q + 1) * CH], False, q == 2 * t + 1)
                close(last, f"y{c}")
            for u in range(2):
                o = open_(f"mean{u}")
                pe.wait_ge(*freed(f"y{2 * u + 1}"))
                close(mm(o[:, :], bones, YT[:, 2 * u:2 * u + 2, :], True, True), f"mean{u}")
            reduce_pairs(["var0", "var1"], bones, YQ, "y_sq")
            for m in range(KD):
                for n in ORDER:
                    name = f"br{m}.{n}"
                    o = open_(name)
                    for k in range(KD):
                        mm3(o[:, 0:T], weights(1), part(H, slice(0, P), k), k == 0, k == KD - 1)
                    if m == 0:
                        ready(pe, "ys_split", 1 if n else 2)
                    for k in range(W4):
                        last = mm3(o[:, T:2 * T], weights(1), part((YH, ys), slice(0, P), n * W4 + k),
                                   k == 0, k == W4 - 1)
                    close(last, name)
            ready(pe, "merged_rest", KD)
            project([f"wo{u}" for u in range(4)], (mgH, mg))

            def ffn(f, rms):
                sum_squares(rms, f"f{f}", sq8)
                a0, s0 = unit[f"up{f}.0"][1], state["slot"]
                assert state["blk"] == 0 and state["A"] == a0

                def up(i, j):
                    ai = a0 + j
                    pe.wait_ge(sem(f"freeA{ai % 4}"), i + ai // 4)
                    for m in range(2):
                        s = s0 + 2 * j + m
                        pe.wait_ge(sem("w_rest"), i * 8 + (s + 1))
                        state["inc"] = True
                        for k in range(KD):
                            if isinstance(i, int) and i == 0 and j == 0 and m == 0:
                                ready(pe, f"h_f{f}", k + 1)
                            c = slice(k * P, (k + 1) * P)
                            last = mm3(psA[ai % 4][:, m * T:(m + 1) * T],
                                       (fr(upper[s % HRING][:, c]), fr(ring[s % RING][:, c])),
                                       part(H, slice(0, P), k), k == 0, k == KD - 1)
                    last.then_inc(sem(f"fullA{ai % 4}"), 1)
                up_loop(pe, up)
                state["slot"], state["A"] = s0 + 2 * UPS, a0 + UPS
                for u in range(KD // 2):
                    name = f"down{f}.{u}"
                    o = open_(name)
                    for m in range(2):
                        for k in range(KF):
                            w = weights(1)
                            if u == 0 and m == 0:
                                ready(pe, "act_ready", f * UPS + k + 1)
                            last = mm3(o[:, m * T:(m + 1) * T], w, part((AH, AL), slice(0, P), k),
                                       k == 0, k == KF - 1)
                    close(last, name)
            ffn(0, "r2")

            sum_squares("r3", "l", sq8)
            project(["lq0", "lq1", "lk0", "lk1"], H, "h_l")
            project_tok(["lv00", "lv01"], H)
            project_tok(["lv10", "lv11"], H)
            o = open_("gt")
            pe.wait_ge(sem("ld_wg"), 16)
            for n in range(2):
                for k in range(KD):
                    for x in H:
                        last = mm(o[0:4, n * T:(n + 1) * T], wgate[:, k, 4 * n:4 * n + 4], rd(x[:, k, :]),
                                  k == 0 and x is HH, k == KD - 1 and x is HL)
            close(last, "gt")
            project([f"lo{u}" for u in range(4)], H)
            o = open_("gcol")
            ready(pe, "g_row")
            for t in range(TT):
                last = mm(o[:, t * 4:t * 4 + 4], rowG[0:4, t * P:(t + 1) * P], ident[0:4, 0:4], True, True)
            close(last, "gcol")
            for h in range(4):
                o = open_(f"mb{h}")
                if h == 0:
                    ready(pe, "m_row")
                close(mm(o[:, :], cst("sel", 4)[:, h * P:(h + 1) * P], rowM2[0:4, :], True, True), f"mb{h}")
                o = open_(f"sc{h}")
                if h == 0:
                    pe.wait_ge(*freed("lk1"))
                mm(o[:, 0:T], lqk[:, 4 + h, 0:P], lqk[:, h, :], True, True)
                close(mm(o[:, T:T + P], lqk[:, 4 + h, P:T], lqk[:, h, P:T], True, True), f"sc{h}")
                o = open_(f"dn{h}")
                pe.wait_ge(*freed(f"sc{h}"))
                s_ = SS[:, h % 2, :]
                mm(o[:, 0:T], ones, s_[:, 0:T], True, False)
                close(mm(o[:, P:T], ones, s_[:, T:T + P], False, True), f"dn{h}")
                o = open_(f"nm{h}")
                if h == 0:
                    pe.wait_ge(*freed("lv11"))
                for e in range(2):
                    es = slice((2 * h + e) * P, (2 * h + e + 1) * P)
                    mm(o[:, e * T:(e + 1) * T], lv[:, 0, es], s_[:, 0:T], True, False)
                    last = mm(o[:, e * T + P:(e + 1) * T], lv[:, 1, es], s_[:, T:T + P], False, True)
                close(last, f"nm{h}")
            for u in range(2):
                o = open_(f"hn{u}")
                ready(pe, "l_sq", u + 1)
                for m in range(2):
                    for e in range(2):
                        last = mm(o[:, m * T:(m + 1) * T], ones, sq2[:, 4 * u + 2 * m + e, :], e == 0, e == 1)
                close(last, f"hn{u}")
            ready(pe, "hr_rest", 4)
            project([f"aw{u}" for u in range(4)], (hrH, hr))
            ffn(1, "r4")

            sum_squares("r5", "a", sq8)
            H2 = (h2H, h2L)
            project([f"bq{u}" for u in range(4)], H2, "h_b")
            project(["bk0", "bk1"], H, "h_a")
            reduce_pairs([f"bqn{u}" for u in range(4)], ones, asq["q"], "a_sq")
            project(["bk2", "bk3"], H)

            def rotate(x, src, n0):
                for u in range(4):
                    o = open_(f"b{x}r{u}")
                    ready(pe, "a_n", n0 + u + 1)
                    close(mm(o[:, :], cst("rot"), src[:, 2 * u:2 * u + 2, :], True, True), f"b{x}r{u}")
            rotate("q", aq, 0)
            project_tok(["bv00", "bv01"], H)
            reduce_pairs([f"bkn{u}" for u in range(4)], ones, asq["k"], "a_sq", 4)
            project_tok(["bv10", "bv11"], H)
            rotate("k", ak, 4)

            def scores(h):
                o = open_(f"as{h}")
                ready(pe, "a_rope", 4 + h // 2 + 1)
                mm(o[:, 0:P], aq[:, h, 0:P], ak[:, h, 0:P], True, True)
                close(mm(o[:, P:3 * P], aq[:, h, P:T], ak[:, h, :], True, True), f"as{h}")
            scores(0)
            scores(1)
            for h in range(8):
                if h < 6:
                    scores(h + 2)
                o = open_(f"at{h}")
                ready(pe, "a_p", h + 1)
                for b, s in enumerate((0, 1, 2)):
                    last = nc.tensor.transpose(o[:, b * P:(b + 1) * P], aP[:, h % 3, s * P:(s + 1) * P], ident)
                close(last, f"at{h}")
                o = open_(f"ao{h}")
                pe.wait_ge(*freed(f"at{h}"))
                if h == 0:
                    pe.wait_ge(*freed("bv11"))
                hs = slice(h * P, (h + 1) * P)
                mm(o[:, 0:T], av[:, 0, hs], aPT[:, h % 2, 0:T], True, False)
                close(mm(o[:, P:T], av[:, 1, hs], aPT[:, h % 2, T:T + P], False, True), f"ao{h}")
            ready(pe, "ao_rest", 8)
            project([f"bo{u}" for u in range(4)], (aoH, ao))
            ffn(2, "r6")
            assert state["A"] == len(LIN) and state["B"] == len(SM)
            assert state["slot"] == ins["w"].shape[0] and state["blk"] == 0

        @block.scalar
        def _(act):
            own = [0]

            def step(ins_):
                own[0] += 1
                ins_.then_inc(sem("act_step"), 1)
                act.wait_ge(sem("act_step"), own[0])

            def split_one(s, use):
                act.wait_ge(sem(f"w{s % RING}"), use * 16)
                A(fr(upper[s % HRING]), ring[s % RING], ACT.Copy).then_inc(sem("w_upper"), 1)

            def split_to(end):
                while split[0] < min(end, nslots):
                    s = split[0]
                    if s >= HRING:
                        ready(act, "slots_used", s - HRING + 1)
                    split_one(s, s // RING + 1)
                    split[0] += 1
            split, nslots = [0], ins["w"].shape[0]

            def take(name):
                if name in SLOT_END:
                    split_to(SLOT_END[name] + 2)
                act.wait_ge(*full(name))
                return bank(name)

            def upper_of(tag, src, dst, n=KD, w=1):
                for k in range(n):
                    ready(act, f"{tag}_f", k + 1)
                    A(fr(dst[:, k * w:(k + 1) * w, :]), src[:, k * w:(k + 1) * w, :], ACT.Copy)\
                        .then_inc(sem(f"{tag}_upper"), 1)

            def release(ins_, name):
                ins_.then_inc(free(name), 1)

            def A(o, i, f, **kw):
                return nc.scalar.activation(o, i, f, **kw)

            def rms(tag, name, src, sq, sd):
                A(sq, src, ACT.Square).then_inc(sem(f"sq_{tag}"), 1)
                o = take(name)
                release(A(sd, o[:, 0:T], ACT.Sqrt, bias=eps6, scale=1.0 / D), name)

            def inverse_root(names, dst, n, s):
                for u, name in enumerate(names):
                    release(A(dst[:, 2 * u:2 * u + 2, :], take(name)[:, :], ACT.Ln, bias=eps6,
                              scale=1.0 / n), name)
                for u, name in enumerate(names):
                    act.wait_ge(*freed(name))
                    c = dst[:, 2 * u:2 * u + 2, :]
                    A(c, c, ACT.Exp, scale=-0.5).then_inc(sem(s), 1)

            act.dma_start(memT, ins["mem"]).then_inc(sem("ld_mem"), 16)
            act.dma_start(par, ins["par"]).then_inc(sem("ld_par"), 16)
            act.dma_start(lora[0:64, 0:512], ins["decay_w2"]).then_inc(sem("ld_lora"), 16)
            act.dma_start(lora[64:128, 0:512], ins["iclr_a2"]).then_inc(sem("ld_lora"), 16)
            act.dma_start(lora[:, 512:1024], ins["gate_g2"]).then_inc(sem("ld_lora"), 16)
            act.dma_start(wgate, ins["wg"]).then_inc(sem("ld_wg"), 16)
            act.wait_ge(sem("ld_x"), 16)
            act.wait_ge(sem("ld_con"), 16)
            rms("x", "rx", xT, sq1, rstd)
            act.wait_ge(sem("ld_mem"), 16)
            rms("m", "rm", memT, sq1, rstdm)
            split_to(4)
            upper_of("h_x", HL, HH)
            upper_of("h_m", memT, memH)
            act.wait_ge(sem("ld_par"), 16)
            ready(act, "omm")
            for u in range(7):
                o = take(f"rw{u}")
                for m in range(2):
                    c = 2 * u + m
                    A(pb[:, c, :], o[:, m * T:(m + 1) * T], ACT.Copy, scale=omm[:, c:c + 1])\
                        .then_inc(sem("shift1"), 1)

            def copy2(name, dst):
                release(A(dst, take(name)[:, :], ACT.Copy), name)
            copy2("sq0", sbqk[:, 0:2, :])
            copy2("sq1", sbqk[:, 2:4, :])
            act.wait_ge(*freed("rw6"))
            split_to(21)
            A(pb[0:64, 12, :], pb[0:64, 12, :], ACT.Tanh).then_inc(sem("lora_in"), 1)
            A(pb[:, 13, :], pb[:, 13, :], ACT.Sigmoid).then_inc(sem("lora_in"), 1)
            for name, dst, b in (("dl", SG, "w0"), ("al", AA, "a0")):
                for u in range(2):
                    o = take(f"{name}{u}")
                    for m in range(2):
                        c = 2 * u + m
                        last = A(dst[:, c, :], o[:, m * T:(m + 1) * T], ACT.Sigmoid, bias=pcol(b, c))
                        if m == 0:
                            last.then_inc(sem("act_aux"), 1)
                    release(last, f"{name}{u}")
            copy2("gl0", GT[:, 0:2, :])
            copy2("gl1", GT[:, 2:4, :])
            for u in range(2):
                release(A(KM[:, 2 * u:2 * u + 2, :], take(f"kn{u}")[:, :], ACT.Sqrt), f"kn{u}")
            copy2("sk0", sbqk[:, 4:6, :])
            copy2("sk1", sbqk[:, 6:8, :])
            ready(act, "cum", 4)
            step(A(GG, LC, ACT.Exp, scale=-DECAY))
            ready(act, "cum_prev")
            A(LC, LC, ACT.Exp, scale=DECAY).then_inc(sem("decays"), 1)
            A(SG, SG, ACT.Exp, scale=-DECAY).then_inc(sem("decays"), 1)
            copy2("sv0", sbv[:, 0, :])
            copy2("sv1", sbv[:, 1, :])
            copy2("mq0", mqk[:, 0:2, :])
            copy2("mq1", mqk[:, 2:4, :])
            copy2("mk0", mqk[:, 4:6, :])
            copy2("mk1", mqk[:, 6:8, :])
            copy2("mv0", mv[:, 0, :])
            copy2("mv1", mv[:, 1, :])
            inverse_root(("sqn0", "sqn1", "skn0", "skn1"), sqs, 64, "sb_inv")
            inverse_root(("mqn0", "mqn1", "mkn0", "mkn1"), sqm, P, "mem_inv")
            split_to(PRE)
            for f in range(2):
                hs = slice(4 * f, 4 * f + 4)
                act.wait_ge(*freed(f"z{4 * f + 3}"))
                ready(act, "mem_n", 4)
                step(A(eb[:, hs, :], zb[:, hs, :], ACT.Abs))
                step(A(eb[:, hs, :], eb[:, hs, :], ACT.Exp, scale=-1.0))
                A(eb[:, hs, :], eb[:, hs, :], ACT.Ln, bias=1.0).then_inc(sem("sb_ln"), 1)
            for f in range(2):
                act.wait_ge(*freed(f"cs{4 * f + 3}"))
                A(zb[:, 4 * f:4 * f + 4, :], zb[:, 4 * f:4 * f + 4, :], ACT.Exp).then_inc(sem("sb_p"), 1)
            for c in range(4):
                o = take(f"so{c}")
                A(ys[0:64, 4 + c, :], o[0:64, 0:T], ACT.Copy).then_inc(sem("act_aux"), 1)
                release(A(ys[64:128, 4 + c, :], o[64:128, T:2 * T], ACT.Copy), f"so{c}")

            def mem_exp(h):
                ready(act, "mem_max", h + 1)
                o = take(f"ms{h}")
                for t in range(TT):
                    last = A(mP[:, h % 2, t * T:(t + 1) * T], o[:, t * T:(t + 1) * T], ACT.Exp,
                             bias=small[:, 24 + 2 * h + t:25 + 2 * h + t], scale=P ** -0.5,
                             accum_out=small[:, 32 + 2 * h + t:33 + 2 * h + t])
                    if t == 0:
                        last.then_inc(sem("act_aux"), 1)
                release(last, f"ms{h}")
            mem_exp(0)
            for h in range(4):
                if h < 3:
                    mem_exp(h + 1)
                copy2(f"mt{h}", mPT[:, h % 2, :])
                release(A(ys[:, 8 + h, :], take(f"mo{h}")[:, 0:T], ACT.Copy), f"mo{h}")
            for t in range(TT):
                for n, name in enumerate("vbka"):
                    name = f"tr{t}.{name}"
                    release(A(tok[:, 4 * t + n, :], take(name)[:, :], ACT.Copy,
                              scale=-1.0 if n == 3 else 1.0), name)
            for t in range(TT):
                copy2(f"mm{t}", MM[:, t, :])
            for g in range(4):
                copy2(f"l0t{g}", XT[:, g, :])
            for l in range(1, 6):
                for g in range(4):
                    copy2(f"l{l}t{g}", XT[:, g, :])
            for t in range(TT):
                copy2(f"zz{t}", ZZ[:, t, :])
            A(fr(YH[:, 4:12, :]), ys[:, 4:12, :], ACT.Copy).then_inc(sem("ys_upper"), 1)
            for c in range(4):
                o = take(f"y{c}")
                A(YT[0:64, c, :], o[0:64, 0:T], ACT.Copy).then_inc(sem("act_aux"), 1)
                release(A(YT[64:128, c, :], o[64:128, T:2 * T], ACT.Copy), f"y{c}")
            for u in range(2):
                release(A(YQ[:, 2 * u:2 * u + 2, :], take(f"var{u}")[:, :], ACT.Sqrt, bias=epsln,
                          scale=1.0 / 64), f"var{u}")
            ready(act, "ys")
            A(fr(YH[:, 0:4, :]), ys[:, 0:4, :], ACT.Copy).then_inc(sem("ys_upper"), 1)
            act.dma_start(xT, ins["x"]).then_inc(sem("ld_x2"), 16)

            def merged_upper(m):
                ready(act, "merged", m + 1)
                A(fr(mgH[:, m, :]), mg[:, m, :], ACT.Copy).then_inc(sem("merged_upper"), 1)
            for i in range(KD * 3):
                name = f"br{i // 3}.{ORDER[i % 3]}"
                if i >= 2:
                    act.wait_ge(*freed(f"br{(i - 2) // 3}.{ORDER[(i - 2) % 3]}"))
                A(sgm[:, i % 2, :], take(name)[:, 0:T], ACT.Sigmoid).then_inc(sem("gate"), 1)
                if i % 3 == 0 and i:
                    merged_upper(i // 3 - 1)
            merged_upper(KD - 1)

            def ffn(f, rms_, xready):
                for u in range(4):
                    split_to(SLOT_END[xready[0] + str(u)] + 2)
                ready(act, xready[1], 4)
                if f == 0:
                    act.dma_start(con2, ins["con"][:, NCON1:NCON]).then_inc(sem("ld_con2"), 16)
                rms(f"f{f}", rms_, xT, sq8, rstd)
                upper_of(f"h_f{f}", HL, HH)
                s0 = SLOT_END[f"up{f}.0"] - 2
                assert split[0] == s0 + 2
                a0 = unit[f"up{f}.0"][1]

                def up(i, j):
                    ai = a0 + j
                    u = i * 4 + j
                    for s in (s0 + 2 * j + 2, s0 + 2 * j + 3):
                        ready(act, "slots_used", i * 8 + (s - HRING + 1))
                        split_one(s, i + (s // RING + 1))
                    act.wait_ge(sem(f"fullA{ai % 4}"), i + ai // 4 + 1)
                    if not (isinstance(i, int) and i == 0 and j < 2):
                        ready(act, "act_ready", u + (f * UPS - 1))
                    for m in range(2):
                        cc = u * 2 + (PCOL[f"cw{f}"] + 4 * KF + m)
                        cb = u * 2 + (PCOL[f"cb{f}"] + m)
                        A(acc[:, j % 2, m * T:(m + 1) * T], psA[ai % 4][:, m * T:(m + 1) * T], ACT.Identity,
                          scale=par[:, bass.ds(cc, 1)], bias=par[:, bass.ds(cb, 1)])\
                            .then_inc(sem("tap2"), 1)
                    ready(act, "conv", u + (f * UPS + 1))
                    A(sil[:, j % 2, :], acc[:, j % 2, 0:T], ACT.Silu).then_inc(sem("silu"), 1)
                up_loop(act, up)
                split[0] = s0 + 2 * UPS + 2

            def after_down(f, x):
                for u in range(4):
                    split_to(SLOT_END[f"down{f}.{u}"] + 2)
                ready(act, x, 4)
            ffn(0, "r2", ("wo", "x1"))

            after_down(0, "x2")
            rms("l", "r3", xT, sq8, rstd)
            upper_of("h_l", HL, HH)
            for n, name in enumerate(("lq0", "lq1")):
                release(A(lqk[:, 2 * n:2 * n + 2, :], take(name)[:, :], ACT.Copy, scale=P ** -0.5), name)
            copy2("lk0", lqk[:, 4:6, :])
            copy2("lk1", lqk[:, 6:8, :])
            for a in range(2):
                for t in range(TT):
                    copy2(f"lv{a}{t}", lv[:, t, a * 512:(a + 1) * 512])
            ready(act, "f_row")
            step(A(rowT[0:4, :], rowLF[0:4, :], ACT.Abs))
            step(A(rowT[0:4, :], rowT[0:4, :], ACT.Exp, scale=-1.0))
            A(rowT[0:4, :], rowT[0:4, :], ACT.Ln, bias=1.0).then_inc(sem("f_ln"), 1)
            for u in range(4):
                release(A(og[:, 2 * u:2 * u + 2, :], take(f"lo{u}")[:, :], ACT.Sigmoid), f"lo{u}")
            split_to(SLOT_END["lo3"] + 3)
            step(A(small[:, 88:96], take("gcol")[:, 0:8], ACT.Copy))
            A(small[:, 96:97], small[:, 88:89], ACT.Copy).then_inc(free("gcol"), 1)
            for h in range(4):
                ready(act, "e_in", h + 1)
                step(A(ET[:, h % 2, 0:T], ET[:, h % 2, 0:T], ACT.Exp, scale=-1.0, bias=small[:, 88 + h:89 + h]))
                A(ET[:, h % 2, T:T + P], ET[:, h % 2, T:T + P], ACT.Exp, scale=-1.0,
                  bias=small[:, 92 + h:93 + h]).then_inc(sem("e_out"), 1)
                if h >= 2:
                    ready(act, "l_den", h - 1)
                release(A(EM[:, h % 2, :], take(f"mb{h}")[:, T:2 * T], ACT.Exp, scale=-1.0), f"mb{h}")
                A(dn[:, h % 2, :], take(f"dn{h}")[:, 0:T], ACT.Abs).then_inc(free(f"dn{h}"), 1)
            for u in range(2):
                release(A(hsd[:, 2 * u:2 * u + 2, :], take(f"hn{u}")[:, :], ACT.Sqrt, bias=eps6,
                          scale=1.0 / T), f"hn{u}")
            upper_of("hr", hr, hrH, 4, 2)
            ffn(1, "r4", ("aw", "x3"))

            after_down(1, "x4")
            rms("a", "r5", xT, sq8, rstd)
            upper_of("h_b", h2L, h2H)
            upper_of("h_a", HL, HH)

            def copies(names, dst):
                for n, d in zip(names, dst):
                    copy2(n, d)
            pair = [slice(2 * u, 2 * u + 2) for u in range(4)]
            copies([f"bq{u}" for u in range(4)], [aq[:, c, :] for c in pair])
            copies(["bk0", "bk1"], [ak[:, c, :] for c in pair[:2]])
            inverse_root([f"bqn{u}" for u in range(4)], asq["q"], P, "a_inv")
            copies(["bk2", "bk3"], [ak[:, c, :] for c in pair[2:]])
            copies(["bv00", "bv01"], [av[:, t, 0:512] for t in range(TT)])
            inverse_root([f"bkn{u}" for u in range(4)], asq["k"], P, "a_inv")
            copies(["bv10", "bv11"], [av[:, t, 512:1024] for t in range(TT)])
            split_to(SLOT_END["bv11"] + 3)

            def a_exp(h):
                ready(act, "a_max", h + 1)
                if h >= 3:
                    act.wait_ge(*freed(f"at{h - 3}"))
                for t in range(TT):
                    s = slice(t * P, 3 * P if t else P)
                    last = A(aP[:, h % 3, s], aS[:, h % 3, s], ACT.Exp,
                             bias=small[:, 56 + 2 * h + t:57 + 2 * h + t], scale=P ** -0.5,
                             accum_out=small[:, 72 + 2 * h + t:73 + 2 * h + t])
                    last.then_inc(sem("a_e"), 1)
            a_exp(0)
            a_exp(1)
            for h in range(8):
                if h < 6:
                    a_exp(h + 2)
                release(A(aPT[:, h % 2, :], take(f"at{h}")[:, 0:384], ACT.Copy), f"at{h}")
                release(A(ao[:, h, :], take(f"ao{h}")[:, 0:T], ACT.Copy), f"ao{h}")
                act.wait_ge(*freed(f"ao{h}"))
                A(fr(aoH[:, h, :]), ao[:, h, :], ACT.Copy).then_inc(sem("ao_upper"), 1)
            ffn(2, "r6", ("bo", "x5"))
            for u in range(4):
                split_to(SLOT_END[f"down2.{u}"] + 2)

        @block.gpsimd
        def _(pool):
            def mul(o, a, b):
                return nc.gpsimd.tensor_tensor(o, a, b, ALU.mult)
            def rest_of(tag, x, upper_, done, n=KD, w=1):
                for k in range(n):
                    ready(pool, f"{tag}_upper", k + 1)
                    c = slice(k * w, (k + 1) * w)
                    nc.gpsimd.tensor_tensor(fr(x[:, c, :]), x[:, c, :], rd(upper_[:, c, :]), ALU.subtract)\
                        .then_inc(sem(done), 1)
            rest_of("h_x", HL, HH, "h_x")
            rest_of("h_m", memT, memH, "h_m")
            ready(pool, "kk_in", 4)
            for u in range(2):
                s = slice(2 * u, 2 * u + 2)
                mul(BN[:, s, :], K1[:, s, :], K1[:, s, :]).then_inc(sem("kk_sq"), 1)
            ready(pool, "cum", 4)
            pool.wait_ge(*freed("dl1"))
            nc.gpsimd.tensor_tensor(SG, LC, SG, ALU.subtract).then_inc(sem("cum_prev"), 1)
            for n, (src, dst, names, s) in enumerate(((sbqk, sqs, ("sq0", "sq1", "sk0", "sk1"), "sb_sq"),
                                                      (mqk, sqm, ("mq0", "mq1", "mk0", "mk1"), "mem_sq"))):
                pool.wait_ge(*freed("mv1"))
                for u, name in enumerate(names):
                    pool.wait_ge(*freed(name))
                    c = slice(2 * u, 2 * u + 2)
                    mul(dst[:, c, :], src[:, c, :], src[:, c, :]).then_inc(sem(s), 1)
            ready(pool, "fm", 3)
            nc.gpsimd.memset(SG, 0.0).then_inc(sem("zeros"), 1)
            nc.gpsimd.memset(view(r0 + 28, 1, 512), 0.0).then_inc(sem("zeros"), 1)
            for g in range(4):
                pool.wait_ge(*freed(f"qd{4 * g + 3}"))
                v = quad[:, 4 * g:4 * g + 4, 0:P]
                nc.gpsimd.tensor_tensor(v, v, bc(ident, 4), ALU.add).then_inc(sem("LT"), 1)
            for u in range(2):
                s = slice(2 * u, 2 * u + 2)
                pool.wait_ge(*freed(f"mean{u}"))
                mul(YQ[:, s, :], YT[:, s, :], YT[:, s, :]).then_inc(sem("y_sq"), 1)

            def ffn(f):
                rest_of(f"h_f{f}", HL, HH, f"h_f{f}")

                def up(i, j):
                    u = i * 4 + j
                    n0 = u * 2 + f * UPS * 2
                    hi, hr_, lr_ = [x[:, bass.ds(u, 1), :].rearrange("p a n -> p (a n)")
                                    for x in (rd(AH), fr(AH), fr(AL))]
                    ready(pool, "silu", u + (f * UPS + 1))
                    mul(gv[:, j % 2, :], sil[:, j % 2, :], acc[:, j % 2, T:2 * T])\
                        .then_inc(sem("act_part"), 1)
                    ready(pool, "act_part", n0 + 1)
                    nc.gpsimd.tensor_copy(hr_, gv[:, j % 2, :]).then_inc(sem("act_part"), 1)
                    ready(pool, "act_part", n0 + 2)
                    nc.gpsimd.tensor_tensor(lr_, gv[:, j % 2, :], hi, ALU.subtract)\
                        .then_inc(sem("act_ready"), 1)
                up_loop(pool, up)
            ffn(0)
            rest_of("h_l", HL, HH, "h_l")
            for u in range(2):
                ready(pool, "l_hr", 4 * u + 4)
                s = slice(4 * u, 4 * u + 4)
                mul(sq2[:, s, :], hr[:, s, :], hr[:, s, :]).then_inc(sem("l_sq"), 1)
            rest_of("hr", hr, hrH, "hr_rest", 4, 2)
            ffn(1)
            rest_of("h_b", h2L, h2H, "h_b")
            rest_of("h_a", HL, HH, "h_a")
            for x, src, n0 in (("q", aq, 0), ("k", ak, 4)):
                for u in range(4):
                    pool.wait_ge(*freed(f"b{x}{u}"))
                    s = slice(2 * u, 2 * u + 2)
                    mul(asq[x][:, s, :], src[:, s, :], src[:, s, :]).then_inc(sem("a_sq"), 1)
                for u in range(4):
                    ready(pool, "a_n", n0 + u + 1)
                    s = slice(2 * u, 2 * u + 2)
                    mul(atm[x][:, s, :], src[:, s, :], bc(cst("cos"), 2)).then_inc(sem("a_cos"), 1)
            rest_of("ao", ao, aoH, "ao_rest")
            ffn(2)

        @block.vector
        def _(dve):
            own = [0]

            def mark(ins_):
                own[0] += 1
                ins_.then_inc(sem("dve_step"), 1)

            def settle():
                dve.wait_ge(sem("dve_step"), own[0])

            def step(ins_):
                mark(ins_)
                settle()

            def split_one(s, done):
                ready(dve, "w_upper", done)
                tt(fr(ring[s % RING]), ring[s % RING], rd(upper[s % HRING]), ALU.subtract)\
                    .then_inc(sem("w_rest"), 1)

            def split_to(end):
                while split[0] < min(end, nslots):
                    split_one(split[0], split[0] + 1)
                    split[0] += 1

            def pump(n=1):
                split_to(min(split[0] + n, PRE))
            split, nslots = [0], ins["w"].shape[0]

            def take(name):
                if name in SLOT_END:
                    split_to(SLOT_END[name] + 2)
                dve.wait_ge(*full(name))
                return bank(name)

            def release(ins_, name):
                ins_.then_inc(free(name), 1)

            V = nc.vector

            def tt(o, a, b, op):
                return V.tensor_tensor(o, a, b, op)

            def stt(o, a, s, b, op0, op1):
                return V.scalar_tensor_tensor(out=o, in0=a, scalar=s, in1=b, op0=op0, op1=op1)

            def norm(tag, name, src, dst, g, sd):
                dve.wait_ge(*freed(name))
                step(V.reciprocal(sd, sd))
                for k in range(KD):
                    stt(dst[:, k, :], src[:, k, :], pcol(g, k), sd, ALU.mult, ALU.mult)\
                        .then_inc(sem(f"h_{tag}_f"), 1)

            dve.wait_ge(sem("ld_par"), 16)
            V.tensor_scalar(omm, par[:, PCOL["mu"]:PCOL["mu"] + 14], -1.0, 1.0, ALU.mult, ALU.add)\
                .then_inc(sem("omm"), 1)
            dve.wait_ge(sem("ld_x"), 16)
            dve.wait_ge(sem("ld_con"), 16)
            norm("x", "rx", xT, HL, "n1", rstd)
            dve.wait_ge(sem("ld_mem"), 16)
            split_to(4)
            norm("m", "rm", memT, memT, "mg", rstdm)
            for u in range(7):
                o = take(f"rw{u}")
                for m in range(2):
                    c = 2 * u + m
                    ready(dve, "shift1", 2 * u + 2)
                    last = stt(pb[:, c, 1:T], o[:, m * T:(m + 1) * T - 1], pcol("mu", c), pb[:, c, 1:T],
                               ALU.mult, ALU.add)
                    if m == 0:
                        mark(last)
                release(last, f"rw{u}")
            settle()
            dve.wait_ge(*freed("rw6"))
            r_, k_, v_ = pb[:, 0:4, :], pb[:, 4:8, :], pb[:, 8:12, :]
            for c in range(4):
                V.tensor_scalar(K1[:, c, :], k_[:, c, :], pcol("kk", c), None, ALU.mult)\
                    .then_inc(sem("kk_in"), 1)
            split_to(21)
            dve.wait_ge(*freed("dl1"))
            for c in range(4):
                V.tensor_tensor_scan(LC[:, c, :], cst("scan"), SG[:, c, :], 0.0, ALU.mult, ALU.add)\
                    .then_inc(sem("cum"), 1)
            for u in range(2):
                dve.wait_ge(*freed(f"kn{u}"))
            step(V.tensor_scalar(KM, KM, 1e-12, None, ALU.max))
            pump(2)
            step(V.reciprocal(KM, KM))
            pump(2)
            step(tt(K1, K1, KM, ALU.mult))
            dve.wait_ge(*freed("al1"))
            ready(dve, "decays", 2)
            mark(tt(AR[:, 0:4, :], K1, SG, ALU.mult))
            pump()
            settle()
            mark(tt(K1, K1, AA, ALU.mult))
            tt(AR[:, 4:8, :], r_, GG, ALU.mult).then_inc(sem("fm"), 1)
            pump()
            settle()
            tt(K1, K1, LC, ALU.mult).then_inc(sem("fm"), 1)
            for c in range(4):
                mark(V.tensor_scalar(AA[:, c, :], AA[:, c, :], -1.0, pcol("ka", c), ALU.add, ALU.mult))
            pump()
            settle()
            pump(2)
            step(stt(KM, AA, 1.0, k_, ALU.add, ALU.mult))
            for c in range(4):
                mark(stt(BN[:, c, :], r_[:, c, :], pcol("rk", c), KM[:, c, :], ALU.mult, ALU.mult))
            pump()
            settle()
            tt(LC, KM, LC, ALU.mult).then_inc(sem("fm"), 1)
            V.memset(small[:, 120:121], 0.0).then_inc(sem("bonus_in"), 1)
            V.memset(small[:, 121:122], 0.0).then_inc(sem("bonus_in"), 1)

            def head_norm(inv, dst, tag, g, n0=0):
                for u in range(4):
                    c = slice(2 * u, 2 * u + 2)
                    ready(dve, f"{tag}_inv", n0 + u + 1)
                    stt(dst[:, c, :], dst[:, c, :], g[u], inv[:, c, :], ALU.mult, ALU.mult)\
                        .then_inc(sem(f"{tag}_n"), 1)
            split_to(PRE)
            head_norm(sqs, sbqk, "sb", [pcol("sbq")] * 2 + [pcol("sbk")] * 2)
            head_norm(sqm, mqk, "mem", [pcol("mq")] * 2 + [pcol("mk")] * 2)
            for u in range(2):
                c = slice(2 * u, 2 * u + 2)
                release(tt(BN[:, c, :], take(f"bon{u}").rearrange("p (c n) -> p c n", c=2), v_[:, c, :],
                           ALU.mult), f"bon{u}")
            ready(dve, "sb_n", 4)
            for h in range(8):
                release(stt(zb[:, h, :], take(f"z{h}")[:, 0:384], 0.125, cst("negS"), ALU.mult, ALU.add),
                        f"z{h}")
            for f in range(2):
                hs = slice(4 * f, 4 * f + 4)
                ready(dve, "sb_ln", f + 1)
                dve.wait_ge(*freed(f"z{4 * f + 3}"))
                stt(eb[:, hs, :], zb[:, hs, :], 0.0, eb[:, hs, :], ALU.max, ALU.add).then_inc(sem("sb_sp"), 1)
            for h in range(8):
                release(tt(zb[:, h, :], zb[:, h, :], take(f"cs{h}")[:, 0:384], ALU.subtract), f"cs{h}")

            def mem_max(h):
                o = take(f"ms{h}")
                mx = small[:, 16 + 2 * h:18 + 2 * h]
                step(V.tensor_reduce(mx, o.rearrange("p (t n) -> p t n", t=2), AX.X, ALU.max))
                V.tensor_scalar(small[:, 24 + 2 * h:26 + 2 * h], mx, -P ** -0.5, None, ALU.mult)\
                    .then_inc(sem("mem_max"), 1)
            mem_max(0)
            for h in range(4):
                if h < 3:
                    mem_max(h + 1)
                dve.wait_ge(*freed(f"ms{h}"))
                rs = small[:, 32 + 2 * h:34 + 2 * h]
                step(V.reciprocal(rs, rs))
                mark(V.tensor_scalar(mP[:, h % 2, 0:T], mP[:, h % 2, 0:T], rs[:, 0:1], None, ALU.mult))
                settle()
                V.tensor_scalar(mP[:, h % 2, T:2 * T], mP[:, h % 2, T:2 * T], rs[:, 1:2], None, ALU.mult)\
                    .then_inc(sem("mem_p"), 1)
            for i in range(16):
                o = take(f"qd{i}")
                mark(tt(quad[:, i, :], o[:, 0:384], cst("mask4")[:, 0:384], ALU.mult))
                settle()
                release(tt(MP[:, i, :], o[:, 384:512], cst("mask4")[:, 384:512], ALU.mult), f"qd{i}")

            def lev(l):
                at = CCOL["lev"][0] + l * P
                return bc(con1[:, at:at + P], 4)

            def four(ap):
                return ap.rearrange("p (i n) -> p i n", i=4)
            for g in range(4):
                release(tt(four(X[:, g, :]), four(take(f"l0x{g}")[:, :]), lev(0), ALU.mult), f"l0x{g}")
            for l in range(1, 6):
                for g in range(4):
                    release(tt(four(T2[:, g, :]), four(take(f"l{l}p{g}")[:, :]), lev(l), ALU.mult),
                            f"l{l}p{g}")
                if l < 5:
                    for g in range(4):
                        release(V.tensor_copy(X[:, g, :], take(f"l{l}x{g}")[:, :]), f"l{l}x{g}")
            for t in range(TT):
                for cp in range(2):
                    name = f"ut{t}.{cp}"
                    o = take(name).rearrange("p (c h n) -> p c h n", c=2, h=2)
                    d = UT[:, 2 * cp:2 * cp + 2, t * P:(t + 1) * P]
                    mark(V.tensor_copy(d[0:64], o[0:64, :, 0, :]))
                    settle()
                    release(V.tensor_copy(d[64:128], o[64:128, :, 1, :]), name)
            ready(dve, "ys_upper", 1)
            tt(fr(ys[:, 4:12, :]), ys[:, 4:12, :], rd(YH[:, 4:12, :]), ALU.subtract).then_inc(sem("ys_split"), 1)
            ready(dve, "zeros", 2)
            for q in range(4):
                t, hs = q // 2, slice(CH * (q % 2), CH * (q % 2) + CH)
                if q == 0:
                    dve.wait_ge(*freed("zz0"))
                    V.tensor_copy(SA[hs, 0, :], ZZ[hs, 0, :]).then_inc(sem("SA0"), 1)
                else:
                    dve.wait_ge(*freed(f"zz{t}"))
                    release(tt(SA[hs, t, :], take(f"sa{q}")[hs, :], ZZ[hs, t, :], ALU.add), f"sa{q}")
                if q < 3:
                    o = take(f"st{q}").rearrange("p (c n) -> p c n", c=4)
                    for r in (0, 64):
                        rs = slice(r, r + 64)
                        d = ST[q + 1][rs, :, rs]
                        gate = GG[rs, :, q * CH + CH - 1:q * CH + CH].to_broadcast([64, 4, 64])
                        src = o[rs, :, rs]
                        if q:
                            step(tt(d, src, ST[q][rs, :, rs], ALU.add))
                            src = d
                        if r and q == 0:
                            release(tt(d, src, gate, ALU.mult), f"st{q}")
                        else:
                            step(tt(d, src, gate, ALU.mult))
                    if q:
                        V.memset(small[:, 122:123], 0.0).then_inc(free(f"st{q}"), 1)
                    else:
                        dve.wait_ge(*freed("st0"))
                    V.memset(small[:, 123:124], 0.0).then_inc(sem("state"), 1)
            for u in range(2):
                c = slice(2 * u, 2 * u + 2)
                release(stt(YT[:, c, :], take(f"mean{u}").rearrange("p (c n) -> p c n", c=2), -1.0 / 64,
                            YT[:, c, :], ALU.mult, ALU.add), f"mean{u}")
            dve.wait_ge(*freed("var1"))
            dve.wait_ge(*freed("var0"))
            step(V.reciprocal(YQ, YQ))
            step(tt(YT, YT, YQ, ALU.mult))
            for c in range(4):
                mark(V.tensor_scalar(YT[:, c, :], YT[:, c, :], pcol("lg", c), pcol("lb", c), ALU.mult, ALU.add))
            settle()
            dve.wait_ge(*freed("bon1"))
            step(tt(YT, YT, BN, ALU.add))
            tt(ys[:, 0:4, :], YT, GT, ALU.mult).then_inc(sem("ys"), 1)
            ready(dve, "ys_upper", 2)
            tt(fr(ys[:, 0:4, :]), ys[:, 0:4, :], rd(YH[:, 0:4, :]), ALU.subtract).then_inc(sem("ys_split"), 1)

            def merged_rest(m):
                ready(dve, "merged_upper", m + 1)
                tt(fr(mg[:, m, :]), mg[:, m, :], rd(mgH[:, m, :]), ALU.subtract).then_inc(sem("merged_rest"), 1)
            for m in range(KD):
                for n in range(3):
                    name = f"br{m}.{ORDER[n]}"
                    o = take(name)
                    ready(dve, "gate", 3 * m + n + 1)
                    g = sgm[:, (3 * m + n) % 2, :]
                    if n == 0:
                        release(tt(mg[:, m, :], g, o[:, T:2 * T], ALU.mult), name)
                        if m:
                            merged_rest(m - 1)
                        dve.wait_ge(*freed(name))
                        continue
                    release(tt(prod, g, o[:, T:2 * T], ALU.mult), name)
                    dve.wait_ge(*freed(name))
                    if n == 1:
                        step(tt(mg[:, m, :], mg[:, m, :], prod, ALU.add))
                    else:
                        tt(mg[:, m, :], mg[:, m, :], prod, ALU.add).then_inc(sem("merged"), 1)
                        ready(dve, "merged", m + 1)
            merged_rest(KD - 1)

            def residual(names, s):
                for u, name in enumerate(names):
                    c = slice(2 * u, 2 * u + 2)
                    step(tt(xT[:, c, :], xT[:, c, :], take(name).rearrange("p (c n) -> p c n", c=2), ALU.add))
                    V.memset(small[:, 124:125], 0.0).then_inc(free(name), 1)
                    V.memset(small[:, 125:126], 0.0).then_inc(sem(s), 1)

            def ffn(f, rms_, g, s):
                norm(f"f{f}", rms_, xT, HL, g, rstd)
                a0, s0 = unit[f"up{f}.0"][1], SLOT_END[f"up{f}.0"] - 2
                assert split[0] == s0 + 2

                def up(i, j):
                    ai = a0 + j
                    u = i * 4 + j
                    for s in (s0 + 2 * j + 2, s0 + 2 * j + 3):
                        split_one(s, i * 8 + (s + 1))
                    dve.wait_ge(sem(f"fullA{ai % 4}"), i + ai // 4 + 1)
                    ready(dve, "tap2", u * 2 + (f * UPS * 2 + 2))
                    for back in (1, 2):
                        for m in range(2):
                            cc = u * 2 + (PCOL[f"cw{f}"] + (2 - back) * 2 * KF + m)
                            d = acc[:, j % 2, m * T + back:(m + 1) * T]
                            last = stt(d, psA[ai % 4][:, m * T:(m + 1) * T - back], par[:, bass.ds(cc, 1)], d,
                                       ALU.mult, ALU.add)
                            last.then_inc(sem(f"taps"), 1)
                        dve.wait_ge(sem("taps"), u * 4 + (f * UPS * 4 + 2 * back))
                    V.memset(small[:, 126:127], 0.0).then_inc(sem(f"freeA{ai % 4}"), 1)
                    V.memset(small[:, 127:128], 0.0).then_inc(sem("conv"), 1)
                up_loop(dve, up)
                split[0] = s0 + 2 * UPS + 2
                residual([f"down{f}.{u}" for u in range(4)], s)
            dve.wait_ge(sem("ld_x2"), 16)
            residual([f"wo{u}" for u in range(4)], "x1")
            ffn(0, "r2", "n2", "x2")

            dve.wait_ge(sem("ld_con2"), 16)
            norm("l", "r3", xT, HL, "an", rstd)
            split_to(SLOT_END["lv11"] + 2)
            o = take("gt")
            mark(V.tensor_scalar(rowG[0:4, :], o[0:4, 0:T], pcol("bi", 0, 4), None, ALU.add))
            settle()
            release(V.tensor_scalar(rowLF[0:4, :], o[0:4, T:2 * T], pcol("bf", 0, 4), None, ALU.add), "gt")
            dve.wait_ge(*freed("gt"))
            V.memset(small[:, 119:120], 0.0).then_inc(sem("f_row"), 1)
            ready(dve, "f_ln")
            step(stt(rowLF[0:4, :], rowLF[0:4, :], 0.0, rowT[0:4, :], ALU.min, ALU.subtract))
            step(V.tensor_tensor_scan(rowF[0:4, :], cst("one", 4), rowLF[0:4, :], 0.0, ALU.mult, ALU.add))
            tt(rowG[0:4, :], rowG[0:4, :], rowF[0:4, :], ALU.subtract).then_inc(sem("g_row"), 1)
            ready(dve, "g_row")
            step(V.tensor_tensor_scan(rowM2[0:4, 0:T], cst("one", 4), rowG[0:4, :], 0.0, ALU.mult, ALU.max))
            tt(rowM2[0:4, T:2 * T], rowM2[0:4, 0:T], rowF[0:4, :], ALU.add).then_inc(sem("m_row"), 1)
            split_to(SLOT_END["lo3"] + 3)
            for h in range(4):
                o = take(f"mb{h}")
                if h >= 2:
                    dve.wait_ge(*freed(f"sc{h - 2}"))
                mark(tt(ET[:, h % 2, 0:T], o[:, 0:T], cst("posI"), ALU.add))
                settle()
                tt(ET[:, h % 2, T:T + P], o[:, P:T], cst("posI")[:, 0:P], ALU.add).then_inc(sem("e_in"), 1)
                ready(dve, "e_out", h + 1)
                release(tt(SS[:, h % 2, :], ET[:, h % 2, :], take(f"sc{h}")[:, 0:384], ALU.mult), f"sc{h}")
                dve.wait_ge(*freed(f"dn{h}"))
                dve.wait_ge(*freed(f"mb{h}"))
                d = dn[:, h % 2, :]
                step(tt(d, d, EM[:, h % 2, :], ALU.max))
                V.reciprocal(d, d).then_inc(sem("l_den"), 1)
                ready(dve, "l_den", h + 1)
                o = take(f"nm{h}")
                for e in range(2):
                    tt(hr[:, 2 * h + e, :], o[:, e * T:(e + 1) * T], d, ALU.mult).then_inc(sem("l_hr"), 1)
                ready(dve, "l_hr", 2 * h + 2)
                V.memset(small[:, 118:119], 0.0).then_inc(free(f"nm{h}"), 1)
            for u in range(2):
                dve.wait_ge(*freed(f"hn{u}"))
                step(V.reciprocal(hsd[:, 2 * u:2 * u + 2, :], hsd[:, 2 * u:2 * u + 2, :]))
            for h in range(4):
                for e in range(2):
                    c = 2 * h + e
                    mark(stt(hr[:, c, :], hr[:, c, :], pcol("ah", c), hsd[:, h, :], ALU.mult, ALU.mult))
            settle()
            for c in range(KD):
                if c % 2 == 0:
                    dve.wait_ge(*freed(f"lo{c // 2}"))
                if c % 2:
                    c2 = slice(c - 1, c + 1)
                    tt(hr[:, c2, :], hr[:, c2, :], og[:, c2, :], ALU.mult).then_inc(sem("hr_f"), 1)
            residual([f"aw{u}" for u in range(4)], "x3")
            ffn(1, "r4", "f0", "x4")

            norm("b", "r5", xT, h2L, "bn", rstd)
            for k in range(KD):
                stt(HL[:, k, :], xT[:, k, :], pcol("kvn", k), rstd, ALU.mult, ALU.mult)\
                    .then_inc(sem("h_a_f"), 1)

            def rope(x, dst, n0, spare, end):
                for u in range(4):
                    c = slice(2 * u, 2 * u + 2)
                    name = f"b{x}r{u}"
                    release(tt(asq[x][:, c, :], take(name).rearrange("p (c n) -> p c n", c=2),
                               bc(cst("sin"), 2), ALU.mult), name)
                    dve.wait_ge(*freed(name))
                    ready(dve, "a_cos", n0 + u + 1)
                    tt(dst[:, c, :], asq[x][:, c, :], atm[x][:, c, :], ALU.add).then_inc(sem("a_rope"), 1)
                    split_to(min(split[0] + spare, end))
            split_to(SLOT_END["bk1"] + 2)
            head_norm(asq["q"], aq, "a", [pcol("bq")] * 4)
            split_to(SLOT_END["bk3"] + 2)
            rope("q", aq, 0, 1, SLOT_END["bv01"] + 2)
            split_to(SLOT_END["bv01"] + 2)
            head_norm(asq["k"], ak, "a", [pcol("kn")] * 4, 4)
            split_to(SLOT_END["bv11"] + 3)
            rope("k", ak, 4, 0, 0)

            def a_max(h):
                if h >= 3:
                    ready(dve, "a_e", 2 * (h - 2))
                o = take(f"as{h}")
                s_ = aS[:, h % 3, :]
                release(tt(s_, o[:, 0:384], cst("negC"), ALU.add), f"as{h}")
                dve.wait_ge(*freed(f"as{h}"))
                mark(V.tensor_reduce(small[:, 40 + 2 * h:41 + 2 * h], s_[:, 0:P], AX.X, ALU.max))
                mark(V.tensor_reduce(small[:, 41 + 2 * h:42 + 2 * h], s_[:, P:3 * P], AX.X, ALU.max))
                settle()
                V.tensor_scalar(small[:, 56 + 2 * h:58 + 2 * h], small[:, 40 + 2 * h:42 + 2 * h], -P ** -0.5,
                                None, ALU.mult).then_inc(sem("a_max"), 1)
            a_max(0)
            a_max(1)
            for h in range(8):
                if h < 6:
                    a_max(h + 2)
                ready(dve, "a_e", 2 * h + 2)
                rs = small[:, 72 + 2 * h:74 + 2 * h]
                step(V.reciprocal(rs, rs))
                p_ = aP[:, h % 3, :]
                step(V.tensor_scalar(p_[:, 0:P], p_[:, 0:P], rs[:, 0:1], None, ALU.mult))
                V.tensor_scalar(p_[:, P:3 * P], p_[:, P:3 * P], rs[:, 1:2], None, ALU.mult)\
                    .then_inc(sem("a_p"), 1)
            residual([f"bo{u}" for u in range(4)], "x5")
            ffn(2, "r6", "f1", "x_final")


def feature_blocks(w):
    k, n = w.shape
    return w.reshape(k // P, P, n // P, P).transpose(2, 0, 1, 3).reshape(-1, P, P)


def token_blocks(w):
    k, n = w.shape
    return w.reshape(k // P, P, n // 512, 4, P).transpose(2, 0, 3, 1, 4).reshape(-1, P, P)


def pairs(w, swap):
    k = w.shape[0]
    v = w.reshape(k, 2, KF, P)
    if swap:
        v = v[:, ::-1]
    return v.transpose(0, 2, 1, 3).reshape(k, 2 * KF * P)


def kernel(**inputs):
    import concourse.bacc as bacc
    from concourse.bass_utils import run_bass_kernel_spmd

    a = {k: np.asarray(v) for k, v in inputs.items() if np.asarray(v).size}
    w_in, kv = a["w_in"][0], a["w_mem_kv"][0]
    cut = np.cumsum([0, 1792, 512, 512, 512, 512, 3072])
    rw, sq, sk, sv, mq, gates = [w_in[:, cut[i]:cut[i + 1]] for i in range(6)]
    g_blocks = feature_blocks(gates).reshape(3, KD, KD, P, P)
    b_blocks = np.stack([feature_blocks(a["w_branch"][0, n]).reshape(KD, W4, P, P) for n in range(3)])
    merge = np.concatenate([g_blocks, b_blocks], 2)[list(ORDER)].transpose(1, 0, 2, 3, 4).reshape(-1, P, P)
    aw = a["a_w_in_2"][0]

    def ffn(up, down, swap):
        return [feature_blocks(pairs(up, swap)), feature_blocks(down)]
    stream = ([feature_blocks(rw), feature_blocks(sq), feature_blocks(sk), token_blocks(sv),
               feature_blocks(mq), feature_blocks(kv[:, :512]), token_blocks(kv[:, 512:]), merge,
               feature_blocks(a["w_out"][0])] + ffn(a["w_up"][0], a["w_down"][0], False)
              + [feature_blocks(aw[:, 0:1024]), token_blocks(aw[:, 1024:2048]),
                 feature_blocks(aw[:, 2048:3072]), feature_blocks(a["a_w_out_2"][0])]
              + ffn(a["f_w_up_2"][0], a["f_w_down_2"][0], True)
              + [feature_blocks(a["b_w_q_2"][0]), feature_blocks(a["w_kv_2"][:, :1024]),
                 token_blocks(a["w_kv_2"][:, 1024:]), feature_blocks(a["b_w_o_2"][0])]
              + ffn(a["f_w_up_2"][1], a["f_w_down_2"][1], True))
    blocks = np.concatenate(stream)
    w = np.ascontiguousarray(blocks.reshape(-1, SLOT, P, P).transpose(0, 2, 1, 3)).reshape(-1, P, SLOT * P)

    par = np.zeros((P, NPAR), np.float32)

    def put(name, v):
        v = np.asarray(v).reshape(-1, P).T
        par[:, PCOL[name]:PCOL[name] + v.shape[1]] = v
    for name, v in (("n1", a["norm1_g"][0]), ("mg", a["mem_norm_g"][0]), ("mu", a["shift_mu"][0]),
                    ("w0", a["decay_w0"][0]), ("a0", a["iclr_a0"][0]), ("kk", a["k_k"][0]),
                    ("ka", a["k_a"][0]), ("rk", a["r_k"][0]), ("lg", a["lnx_g"][0]), ("lb", a["lnx_b"][0]),
                    ("sbq", np.tile(a["sb_q_norm_g"][0], 2)), ("sbk", np.tile(a["sb_k_norm_g"][0], 2)),
                    ("mq", a["mem_q_norm_g"][0]), ("mk", a["mem_k_norm_g"][0]), ("n2", a["norm2_g"][0]),
                    ("an", a["a_norm_2"][0]), ("ah", a["a_h_norm_2"][0]), ("kvn", a["kv_norm_2"]),
                    ("kn", a["k_norm_2"]), ("bn", a["b_norm_2"][0]), ("bq", a["b_q_norm_2"][0]),
                    ("f0", a["f_norm_2"][0]), ("f1", a["f_norm_2"][1])):
        put(name, v)
    par[0:4, PCOL["bi"]] = a["a_b_gates_2"][0, 0]
    par[0:4, PCOL["bf"]] = a["a_b_gates_2"][0, 1]
    for f, (cw, cb, swap) in enumerate(((a["conv_w"][0], a["conv_b"][0], False),
                                        (a["f_conv_w_2"][0], a["f_conv_b_2"][0], True),
                                        (a["f_conv_w_2"][1], a["f_conv_b_2"][1], True))):
        put(f"cw{f}", pairs(cw, swap))
        put(f"cb{f}", pairs(cb[None], swap))

    def major(v):
        return np.ascontiguousarray(v.T.reshape(-1, P, v.shape[0]).transpose(1, 0, 2))
    arrays = {
        "x": major(a["x"][0]), "mem": major(a["mem"][0]), "w": w, "par": par, "con": constants(),
        "decay_w2": a["decay_w2"][0], "iclr_a2": a["iclr_a2"][0], "gate_g2": a["gate_g2"][0],
        "wg": np.ascontiguousarray(aw[:, 3072:3080].reshape(KD, P, 8).transpose(1, 0, 2)),
    }
    arrays = {f"in_{k}": np.ascontiguousarray(v) for k, v in arrays.items()}
    nc = bacc.Bacc("TRN2", target_bir_lowering=False, num_devices=1)
    ins = {k[3:]: nc.dram_tensor(k, v.shape, F32, kind="ExternalInput").ap() for k, v in arrays.items()}
    out = nc.dram_tensor("out", (P, KD, T), F32, kind="ExternalOutput").ap()
    program(nc, ins, out)
    r = run_bass_kernel_spmd(nc, [arrays], core_ids=[0]).results[0]["out"]
    return r.reshape(P, KD, T).transpose(2, 1, 0).reshape(1, T, D)
```
